# Optimizing a Trainium2 kernel written in Bass

```python
import math
import jax, jax.numpy as jnp
from jax import lax
import numpy as np
import jax
import jax.numpy as jnp

D_MODEL = 1024
BATCH = 1
SEQ = 512
DEPTH = 2

CHUNK = 64
QBLK = 128
POOL_WIDTH = D_MODEL
POOL_GROUPS = 4
POOL_GROUP = POOL_WIDTH // POOL_GROUPS
POOL_WINDOWS = (2, 4, 8, 16)
DIFF_QK_DIM = 128
DIFF_V_DIM = 2 * DIFF_QK_DIM
DIFF_HEADS = D_MODEL // DIFF_V_DIM
DIFF_QK_WIDTH = DIFF_HEADS * 2 * DIFF_QK_DIM
DIFF_V_WIDTH = DIFF_HEADS * DIFF_V_DIM
ROT_DIM = DIFF_QK_DIM // 4
ROPE_THETA = 500000.0
N_BRANCHES = 2
IN_WIDTH = POOL_WIDTH + 2 * DIFF_QK_WIDTH + DIFF_V_WIDTH + N_BRANCHES * D_MODEL
FFN_HIDDEN = -(-8 * D_MODEL // (3 * 256)) * 256
NORM_EPS = 1e-6


def rmsnorm(x, g):
    xf = x.astype(jnp.float32)
    y = xf * lax.rsqrt(jnp.mean(xf * xf, axis=-1, keepdims=True) + NORM_EPS)
    return (y * g.astype(jnp.float32)).astype(x.dtype)

def rotary_tables(seq, dtype):
    pos = jnp.arange(seq, dtype=jnp.float32)
    inv_freq = ROPE_THETA ** (-jnp.arange(0, ROT_DIM, 2, dtype=jnp.float32) / ROT_DIM)
    ang = pos[:, None] * inv_freq[None, :]
    return jnp.cos(ang).astype(dtype), jnp.sin(ang).astype(dtype)

def apply_partial_rotary(t, cos, sin):
    half = ROT_DIM // 2
    t1, t2, rest = t[..., :half], t[..., half:ROT_DIM], t[..., ROT_DIM:]
    return jnp.concatenate([t1 * cos - t2 * sin, t2 * cos + t1 * sin, rest], axis=-1)

def pool_mixer(u, w_pool, scale):
    b, s, _ = u.shape
    ug = u.reshape(b, s, POOL_GROUPS, POOL_GROUP)
    t_idx = jnp.arange(s, dtype=jnp.float32)[None, :, None]
    outs = []
    for gi, w in enumerate(POOL_WINDOWS):
        xg = ug[:, :, gi, :].astype(jnp.float32)
        c = jnp.cumsum(xg, axis=1)
        c_shift = jnp.pad(c, ((0, 0), (w, 0), (0, 0)))[:, :s]
        count = jnp.minimum(t_idx + 1.0, float(w))
        outs.append((c - c_shift) / count - xg)
    pooled = jnp.stack(outs, axis=2).astype(u.dtype)
    y = jnp.einsum('bsgc,gcd->bsgd', pooled, w_pool)
    return y.reshape(b, s, POOL_WIDTH) * scale

def diff_attention(q, k, v, lam):
    b, h, _, s, d = q.shape
    nblk = s // QBLK
    chunk_ids = jnp.arange(s) // CHUNK
    qb = q.reshape(b, h, 2, nblk, QBLK, d).transpose(3, 0, 1, 2, 4, 5)
    qc = chunk_ids.reshape(nblk, QBLK)
    scale = DIFF_QK_DIM ** -0.5
    neg = jnp.finfo(jnp.float32).min

    def one_block(args):
        qi, ci = args
        sc = jnp.einsum('bhcqd,bhckd->bhcqk', qi, k).astype(jnp.float32) * scale
        mask = ci[:, None] >= chunk_ids[None, :]
        p = jax.nn.softmax(jnp.where(mask, sc, neg), axis=-1)
        a = p[:, :, 0] - lam * p[:, :, 1]
        return jnp.einsum('bhqk,bhkv->bhqv', a.astype(v.dtype), v)

    out = lax.map(one_block, (qb, qc))
    return out.transpose(1, 2, 0, 3, 4).reshape(b, h, s, DIFF_V_DIM)

def first_inputs(seed: int = 0) -> dict:
    key = jax.random.key(seed)
    ks = jax.random.split(key, 16)
    f32 = jnp.float32
    nrm = lambda k, shp, std: jax.random.normal(k, shp, f32) * std
    return {
        "x": jax.random.normal(ks[0], (BATCH, SEQ, D_MODEL), f32),
        "norm1_g": 1.0 + nrm(ks[1], (DEPTH, D_MODEL), 0.02),
        "w_in": nrm(ks[2], (DEPTH, D_MODEL, IN_WIDTH), D_MODEL ** -0.5),
        "q_norm_g": 1.0 + nrm(ks[3], (DEPTH, DIFF_QK_DIM), 0.02),
        "k_norm_g": 1.0 + nrm(ks[4], (DEPTH, DIFF_QK_DIM), 0.02),
        "lam_q1": nrm(ks[5], (DEPTH, DIFF_QK_DIM), 0.1),
        "lam_k1": nrm(ks[6], (DEPTH, DIFF_QK_DIM), 0.1),
        "lam_q2": nrm(ks[7], (DEPTH, DIFF_QK_DIM), 0.1),
        "lam_k2": nrm(ks[8], (DEPTH, DIFF_QK_DIM), 0.1),
        "subln_g": 1.0 + nrm(ks[9], (DEPTH, DIFF_V_DIM), 0.02),
        "pool_w": nrm(ks[10], (DEPTH, POOL_GROUPS, POOL_GROUP, POOL_GROUP), POOL_GROUP ** -0.5),
        "pool_scale": 1.0 + nrm(ks[11], (DEPTH, POOL_WIDTH), 0.02),
        "w_out": nrm(ks[12], (DEPTH, D_MODEL, D_MODEL), D_MODEL ** -0.5),
        "norm2_g": 1.0 + nrm(ks[13], (DEPTH, D_MODEL), 0.02),
        "w_ffn_in": nrm(ks[14], (DEPTH, D_MODEL, 2 * FFN_HIDDEN), D_MODEL ** -0.5),
        "w_ffn_out": nrm(ks[15], (DEPTH, FFN_HIDDEN, D_MODEL), FFN_HIDDEN ** -0.5),
    }

def first_block(x, norm1_g, w_in, q_norm_g, k_norm_g, lam_q1, lam_k1, lam_q2, lam_k2,
              subln_g, pool_w, pool_scale, w_out, norm2_g, w_ffn_in, w_ffn_out):
    b, s, _ = x.shape
    cos, sin = rotary_tables(s, x.dtype)
    splits = np.cumsum([POOL_WIDTH, DIFF_QK_WIDTH, DIFF_QK_WIDTH, DIFF_V_WIDTH, D_MODEL]).tolist()
    for i in range(DEPTH):
        lam_init = 0.8 - 0.6 * math.exp(-0.3 * i)
        xn = rmsnorm(x, norm1_g[i])
        proj = xn @ w_in[i]
        u_pool, q, k, v, g_a, g_b = jnp.split(proj, splits, axis=-1)
        q = q.reshape(b, s, DIFF_HEADS, 2, DIFF_QK_DIM).transpose(0, 2, 3, 1, 4)
        k = k.reshape(b, s, DIFF_HEADS, 2, DIFF_QK_DIM).transpose(0, 2, 3, 1, 4)
        q = apply_partial_rotary(rmsnorm(q, q_norm_g[i]), cos, sin)
        k = apply_partial_rotary(rmsnorm(k, k_norm_g[i]), cos, sin)
        v = v.reshape(b, s, DIFF_HEADS, DIFF_V_DIM).transpose(0, 2, 1, 3)
        lam = (jnp.exp(jnp.sum(lam_q1[i].astype(jnp.float32) * lam_k1[i].astype(jnp.float32)))
               - jnp.exp(jnp.sum(lam_q2[i].astype(jnp.float32) * lam_k2[i].astype(jnp.float32)))
               + lam_init)
        o = diff_attention(q, k, v, lam)
        o = rmsnorm(o, subln_g[i]) * (1.0 - lam_init)
        attn_out = o.transpose(0, 2, 1, 3).reshape(b, s, DIFF_V_WIDTH)
        pool_out = pool_mixer(u_pool, pool_w[i], pool_scale[i])
        merged = jax.nn.sigmoid(g_a) * pool_out + jax.nn.sigmoid(g_b) * attn_out
        x = x + merged @ w_out[i]
        hn = rmsnorm(x, norm2_g[i])
        gate, up = jnp.split(hn @ w_ffn_in[i], 2, axis=-1)
        x = x + (jax.nn.silu(gate) * up) @ w_ffn_out[i]
    return x


DEPTH_2 = 1

HEAD_DIM = 64
ROPE_THETA_2 = 10000.0
RMS_EPS = 1e-6
Q_BLOCK = 128

A_HEADS = 8
A_KV_HEADS = 2
IDX_HEADS = 4
IDX_DIM = 64
TOPK_MAX = 256

B_PATTERNS = ((128, 1), (512, 4), (2048, 16))
B_N_GROUPS = 3
B_HEADS = 8

MEM_LEN = 256
M_HEADS = 4
M_HEAD_DIM = 128

BRANCH_WIDTH = 512
N_BRANCHES_2 = 3

MOE_GROUPS = 4
EXPERTS_PER_GROUP = 4
N_EXPERTS = 16
MOE_TOPK = 2
EXPERT_HIDDEN = 512

IN_SPLITS = (512, 128, 128, 256, 64, 4, 1536, 1536, 1536, 512)
IN_WIDTH_2 = 6212


def rmsnorm_2(x, g):
    xf = x.astype(jnp.float32)
    y = xf * lax.rsqrt(jnp.mean(xf * xf, axis=-1, keepdims=True) + RMS_EPS)
    return (y * g.astype(jnp.float32)).astype(x.dtype)

def rope(x):
    s, dh = x.shape[1], x.shape[-1]
    half = dh // 2
    inv = ROPE_THETA_2 ** (-jnp.arange(half, dtype=jnp.float32) / half)
    ang = jnp.arange(s, dtype=jnp.float32)[:, None] * inv[None, :]
    cos = jnp.cos(ang)[None, :, None, :]
    sin = jnp.sin(ang)[None, :, None, :]
    xf = x.astype(jnp.float32)
    x1, x2 = xf[..., :half], xf[..., half:]
    return jnp.concatenate([x1 * cos - x2 * sin, x2 * cos + x1 * sin], axis=-1).astype(x.dtype)

def split_cols(a, sizes):
    out, off = [], 0
    for n in sizes:
        out.append(a[..., off:off + n])
        off += n
    return out

def sweep_query_blocks(fn, seq_len):
    out = lax.map(fn, jnp.arange(seq_len // Q_BLOCK))
    nb, b = out.shape[0], out.shape[1]
    return jnp.moveaxis(out, 0, 1).reshape(b, nb * Q_BLOCK, *out.shape[3:])

def dsa_attention(q, k, v, q_idx, k_idx, w_idx):
    b, s, h, dh = q.shape
    kvh = k.shape[2]
    g = h // kvh
    topk = min(TOPK_MAX, s // 4)
    key_pos = jnp.arange(s)
    local = jnp.arange(Q_BLOCK)
    k_idx_f = k_idx.astype(jnp.float32)

    def block(i):
        q0 = i * Q_BLOCK
        qpos = q0 + local
        qi = lax.dynamic_slice_in_dim(q_idx, q0, Q_BLOCK, axis=1).astype(jnp.float32)
        wi = lax.dynamic_slice_in_dim(w_idx, q0, Q_BLOCK, axis=1).astype(jnp.float32)
        dots = jnp.einsum('bqhd,bsd->bqhs', qi, k_idx_f) * (IDX_DIM ** -0.5)
        score = jnp.einsum('bqhs,bqh->bqs', jax.nn.relu(dots), wi) * (IDX_HEADS ** -0.5)
        causal = key_pos[None, :] <= qpos[:, None]
        score = jnp.where(causal[None], score, -jnp.inf)
        _, sel = lax.top_k(score, topk)
        valid = sel <= qpos[None, :, None]
        ks = jax.vmap(lambda kk, ii: kk[ii])(k, sel)
        vs = jax.vmap(lambda vv, ii: vv[ii])(v, sel)
        qb = lax.dynamic_slice_in_dim(q, q0, Q_BLOCK, axis=1).reshape(b, Q_BLOCK, kvh, g, dh)
        logits = jnp.einsum('bqkgd,bqjkd->bqkgj', qb, ks).astype(jnp.float32) * (dh ** -0.5)
        logits = jnp.where(valid[:, :, None, None, :], logits, -jnp.inf)
        p = jax.nn.softmax(logits, axis=-1)
        o = jnp.einsum('bqkgj,bqjkd->bqkgd', p.astype(vs.dtype), vs)
        return o.reshape(b, Q_BLOCK, h * dh)

    return sweep_query_blocks(block, s)

def dilated_attention(q, k, v):
    b, s, ng, h, dh = q.shape
    local = jnp.arange(Q_BLOCK)
    qs = [q[:, :, gi] for gi in range(ng)]
    kp = [jnp.pad(k[:, :, gi], ((0, 0), (w, 0), (0, 0), (0, 0))) for gi, (w, _) in enumerate(B_PATTERNS)]
    vp = [jnp.pad(v[:, :, gi], ((0, 0), (w, 0), (0, 0), (0, 0))) for gi, (w, _) in enumerate(B_PATTERNS)]

    def block(i):
        q0 = i * Q_BLOCK
        outs, lses = [], []
        for gi, (window, dil) in enumerate(B_PATTERNS):
            steps = jnp.arange(window // dil + 1)
            back = local[:, None] - steps[None, :] * dil
            valid = (q0 + back) >= 0
            rel = window + back
            ks = lax.dynamic_slice_in_dim(kp[gi], q0, window + Q_BLOCK, axis=1)[:, rel]
            vs = lax.dynamic_slice_in_dim(vp[gi], q0, window + Q_BLOCK, axis=1)[:, rel]
            qg = lax.dynamic_slice_in_dim(qs[gi], q0, Q_BLOCK, axis=1)
            logits = jnp.einsum('bqhd,bqjhd->bqhj', qg, ks).astype(jnp.float32) * (dh ** -0.5)
            logits = jnp.where(valid[None, :, None, :], logits, -jnp.inf)
            lse = jax.nn.logsumexp(logits, axis=-1)
            p = jnp.exp(logits - lse[..., None])
            outs.append(jnp.einsum('bqhj,bqjhd->bqhd', p.astype(vs.dtype), vs))
            lses.append(lse)
        alpha = jax.nn.softmax(jnp.stack(lses, axis=2), axis=2)
        o = jnp.einsum('bqgh,bqghd->bqhd', alpha.astype(outs[0].dtype), jnp.stack(outs, axis=2))
        return o.reshape(b, Q_BLOCK, h * dh)

    return sweep_query_blocks(block, s)

def memory_attention(qm, mem_n, w_mem_kv):
    b, m, _ = mem_n.shape
    km, vm = split_cols(mem_n @ w_mem_kv, (M_HEADS * M_HEAD_DIM, M_HEADS * M_HEAD_DIM))
    km = km.reshape(b, m, M_HEADS, M_HEAD_DIM)
    vm = vm.reshape(b, m, M_HEADS, M_HEAD_DIM)
    logits = jnp.einsum('bshd,bmhd->bhsm', qm, km).astype(jnp.float32) * (M_HEAD_DIM ** -0.5)
    p = jax.nn.softmax(logits, axis=-1)
    o = jnp.einsum('bhsm,bmhd->bshd', p.astype(vm.dtype), vm)
    return o.reshape(b, qm.shape[1], M_HEADS * M_HEAD_DIM)

def hier_moe(xn, w_group, b_group, w_sub, b_sub, w1, w3, w2):
    b, s, d = xn.shape
    t = xn.reshape(b * s, d)
    gl = (t @ w_group).astype(jnp.float32) + b_group.astype(jnp.float32)
    gp = jax.nn.softmax(gl, axis=-1)
    g_w, g_sel = lax.top_k(gp, 1)
    sl = jnp.einsum('td,gde->tge', t, w_sub).astype(jnp.float32) + b_sub.astype(jnp.float32)
    sl = jnp.take_along_axis(sl, g_sel[:, :, None], axis=1)[:, 0]
    sp = jax.nn.softmax(sl, axis=-1)
    top_p, top_e = lax.top_k(sp, MOE_TOPK)
    top_p = top_p / jnp.sum(top_p, axis=-1, keepdims=True)
    expert_id = g_sel * EXPERTS_PER_GROUP + top_e
    combine = jnp.einsum('tk,tke->te', g_w * top_p, jax.nn.one_hot(expert_id, N_EXPERTS, dtype=jnp.float32))
    out = jnp.zeros((b * s, d), jnp.float32)
    for e in range(N_EXPERTS):
        hid = jax.nn.silu(t @ w1[e]) * (t @ w3[e])
        out = out + combine[:, e:e + 1] * (hid @ w2[e]).astype(jnp.float32)
    return out.astype(xn.dtype).reshape(b, s, d)

def second_inputs(seed: int = 0) -> dict:
    key = jax.random.key(seed)
    ks = jax.random.split(key, 19)
    f32 = jnp.float32
    L, D = DEPTH_2, D_MODEL

    def dense(k, shape, fan_in):
        return jax.random.normal(k, shape, f32) * (fan_in ** -0.5)

    def gain(k, shape):
        return 1.0 + 0.02 * jax.random.normal(k, shape, f32)

    def small(k, shape, scale):
        return scale * jax.random.normal(k, shape, f32)

    return {
        'x': jax.random.normal(ks[0], (BATCH, SEQ, D), f32),
        'mem': jax.random.normal(ks[1], (BATCH, MEM_LEN, D), f32),
        'g_mix': gain(ks[2], (L, D)),
        'g_mem': gain(ks[3], (L, D)),
        'w_in': dense(ks[4], (L, D, IN_WIDTH_2), D),
        'w_mem_kv': dense(ks[5], (L, D, 2 * M_HEADS * M_HEAD_DIM), D),
        'w_gate': dense(ks[6], (L, D, N_BRANCHES_2 * D), D),
        'b_gate': small(ks[7], (L, N_BRANCHES_2 * D), 0.1),
        'w_branch': dense(ks[8], (L, N_BRANCHES_2, BRANCH_WIDTH, D), BRANCH_WIDTH),
        'w_out': dense(ks[9], (L, D, D), D),
        'g_ffn': gain(ks[10], (L, D)),
        'w_group': dense(ks[11], (L, D, MOE_GROUPS), D),
        'b_group': small(ks[12], (L, MOE_GROUPS), 0.01),
        'w_sub': dense(ks[13], (L, MOE_GROUPS, D, EXPERTS_PER_GROUP), D),
        'b_sub': small(ks[14], (L, MOE_GROUPS, EXPERTS_PER_GROUP), 0.01),
        'w1': dense(ks[15], (L, N_EXPERTS, D, EXPERT_HIDDEN), D),
        'w3': dense(ks[16], (L, N_EXPERTS, D, EXPERT_HIDDEN), D),
        'w2': dense(ks[17], (L, N_EXPERTS, EXPERT_HIDDEN, D), EXPERT_HIDDEN),
        'g_final': gain(ks[18], (D,)),
    }

def second_block(x, mem, g_mix, g_mem, w_in, w_mem_kv, w_gate, b_gate, w_branch, w_out, g_ffn,
              w_group, b_group, w_sub, b_sub, w1, w3, w2, g_final):
    b, s, d = x.shape
    h = x
    for l in range(DEPTH_2):
        n = rmsnorm_2(h, g_mix[l])
        aq, ak, av, iq, ik, iw, bq, bk, bv, mq = split_cols(n @ w_in[l], IN_SPLITS)
        aq = rope(aq.reshape(b, s, A_HEADS, HEAD_DIM))
        ak = rope(ak.reshape(b, s, A_KV_HEADS, HEAD_DIM))
        av = av.reshape(b, s, A_KV_HEADS, HEAD_DIM)
        iq = rope(iq.reshape(b, s, IDX_HEADS, IDX_DIM))
        ik = rope(ik.reshape(b, s, 1, IDX_DIM))[:, :, 0]
        y_a = dsa_attention(aq, ak, av, iq, ik, iw)
        bq = rope(bq.reshape(b, s, B_N_GROUPS * B_HEADS, HEAD_DIM)).reshape(b, s, B_N_GROUPS, B_HEADS, HEAD_DIM)
        bk = rope(bk.reshape(b, s, B_N_GROUPS * B_HEADS, HEAD_DIM)).reshape(b, s, B_N_GROUPS, B_HEADS, HEAD_DIM)
        bv = bv.reshape(b, s, B_N_GROUPS, B_HEADS, HEAD_DIM)
        y_b = dilated_attention(bq, bk, bv)
        y_m = memory_attention(mq.reshape(b, s, M_HEADS, M_HEAD_DIM), rmsnorm_2(mem, g_mem[l]), w_mem_kv[l])
        gates = jax.nn.sigmoid((n @ w_gate[l] + b_gate[l]).astype(jnp.float32)).astype(n.dtype)
        gates = gates.reshape(b, s, N_BRANCHES_2, d)
        merged = (gates[:, :, 0] * (y_a @ w_branch[l, 0])
                  + gates[:, :, 1] * (y_b @ w_branch[l, 1])
                  + gates[:, :, 2] * (y_m @ w_branch[l, 2]))
        h = h + merged @ w_out[l]
        h = h + hier_moe(rmsnorm_2(h, g_ffn[l]), w_group[l], b_group[l], w_sub[l], b_sub[l], w1[l], w3[l], w2[l])
    return rmsnorm_2(h, g_final)


def setup_inputs(seed=0):
    out = dict(first_inputs(seed))
    for name, value in second_inputs(seed + 1).items():
        if name != "x":
            out[name + "_2"] = value
    return out


def reference(
    x, norm1_g, w_in, q_norm_g, k_norm_g, lam_q1, lam_k1, lam_q2, lam_k2, subln_g, pool_w,
    pool_scale, w_out, norm2_g, w_ffn_in, w_ffn_out, mem_2, g_mix_2, g_mem_2, w_in_2,
    w_mem_kv_2, w_gate_2, b_gate_2, w_branch_2, w_out_2, g_ffn_2, w_group_2, b_group_2, w_sub_2,
    b_sub_2, w1_2, w3_2, w2_2, g_final_2,
):
    x = first_block(
        x, norm1_g, w_in, q_norm_g, k_norm_g, lam_q1, lam_k1, lam_q2, lam_k2, subln_g, pool_w,
        pool_scale, w_out, norm2_g, w_ffn_in, w_ffn_out,
    )
    return second_block(
        x, mem_2, g_mix_2, g_mem_2, w_in_2, w_mem_kv_2, w_gate_2, b_gate_2, w_branch_2, w_out_2,
        g_ffn_2, w_group_2, b_group_2, w_sub_2, b_sub_2, w1_2, w3_2, w2_2, g_final_2,
    )


_drawn_inputs = setup_inputs


def setup_inputs(seed=0):
    import zlib

    import numpy as np

    out = dict(_drawn_inputs(seed))
    spreads = {}
    factors = {'q_norm_g': 3.337,
     'k_norm_g': 3.983,
     'lam_k2': 2.944,
     'subln_g': 3.082,
     'pool_scale': 3.22,
     'g_mix_2': 4.435,
     'g_mem_2': 7.442,
     'b_gate_2': 4.435,
     'g_ffn_2': 3.378,
     'b_group_2': 8.0,
     'b_sub_2': 6.479,
     'g_final_2': 2.788}
    for name, (base, spread) in spreads.items():
        noise = np.random.default_rng([zlib.crc32(name.encode()), seed]).standard_normal(out[name].shape)
        drawn = base * np.exp(spread * noise) if base else spread * noise
        out[name] = jnp.asarray(drawn.astype(out[name].dtype))
    for name, factor in factors.items():
        out[name] = (out[name] * factor).astype(out[name].dtype)
    return out
```

```python
from contextlib import ExitStack
from math import exp as math_exp

import numpy as np
import concourse.bass as bass
from concourse import mybir

F32 = mybir.dt.float32
F32R = mybir.dt.float32r
ALU = mybir.AluOpType
ACT = mybir.ActivationFunctionType
AX = mybir.AxisListType

P = 128
SEQ = 512
TOK = SEQ // P
D = 1024
KT = D // P
LAYERS = 2
CHUNK = 64
EPS = 1e-6
NEG = -1e30

DH1 = 128
HEADS1 = 4
VD1 = 256
ROT_HALF = 16
SCALE1 = DH1 ** -0.5
POOL_WINDOWS = (2, 4, 8, 16)
HID1 = 2816
GROUPS1 = HID1 // 256

DH2 = 64
SCALE2 = DH2 ** -0.5
SCALE_M = 128 ** -0.5
MEM = 256
TOPK = 128
PICKED = -3e38
EXPERTS = 16
HID2 = 512
GROUPS2 = EXPERTS * HID2 // 256
AQ, AK, AV, IQ, IK, IW, BQ, BK, BV, MQ = 0, 512, 640, 768, 1024, 1088, 1092, 2628, 4164, 5700

RING = 3
UNIT = 2048
LAYER_UNITS = 2 * 12 + 1 + 2 * 2 + 3 * GROUPS1
NARROW_UNIT = LAYERS * LAYER_UNITS + 3 * 6 + 6 + 2
TOTAL_UNITS = NARROW_UNIT + 1 + 2 + 6 + 6 + 6 + 4 + 3 * GROUPS2


def host_constants():
    pos = np.arange(SEQ, dtype=np.float32)

    def table(theta, half, width):
        e = (np.arange(half, dtype=np.float32) * np.float32(1.0)) / np.float32(half)
        inv = (np.float32(theta) ** (-e)).astype(np.float32)
        ang = (pos[:, None] * inv[None, :]).astype(np.float32)
        return np.cos(ang).astype(np.float32), np.sin(ang).astype(np.float32)

    def tiles(a):
        return np.ascontiguousarray(a.reshape(TOK, P, -1).transpose(1, 0, 2))

    c1, s1 = table(500000.0, ROT_HALF, 16)
    c2, s2 = table(10000.0, DH2 // 2, 32)
    rope1 = np.concatenate([tiles(c1), tiles(s1)], axis=2)
    rope2 = np.concatenate([tiles(np.concatenate([c2, c2], 1)), tiles(np.concatenate([-s2, s2], 1))], axis=2)
    q, k = np.arange(P)[:, None], np.arange(P)[None, :]
    neg = lambda keep: np.where(keep, 0.0, NEG).astype(np.float32)
    causal = neg(k <= q)
    free = np.zeros((P, P), np.float32)
    m4, m16 = neg((q - k) % 4 == 0), neg((q - k) % 16 == 0)
    masks = np.stack([
        np.concatenate([free, free, neg(k >= q), causal], 1),
        np.concatenate([m4, m4, m4, neg(((q - k) % 4 == 0) & (k <= q))], 1),
        np.concatenate([m16, m16, m16, neg(((q - k) % 16 == 0) & (k <= q))], 1),
        np.concatenate([free, free, free, causal], 1),
    ]).astype(np.float32)
    chunk = neg(q // CHUNK >= k // CHUNK)
    count = np.stack([1.0 / np.minimum(pos + 1.0, float(w)) for w in POOL_WINDOWS]).astype(np.float32)
    lam = np.array([[0.8 - 0.6 * math_exp(-0.3 * i), 1.0 - (0.8 - 0.6 * math_exp(-0.3 * i))]
                    for i in range(LAYERS)], np.float32)
    return {"c_ident": np.eye(P, dtype=np.float32), "c_rope1": rope1, "c_rope2": rope2, "c_masks": masks,
            "c_chunk": chunk, "c_count": count, "c_lam": lam}


def build(nc, A, out):
    with ExitStack() as ctx:
        def sb(name, shape, dt=F32):
            return ctx.enter_context(nc.sbuf_tensor(name, shape, dt))

        def sem(name):
            return ctx.enter_context(nc.semaphore(name))

        def at(kb, name, shape, dt=F32):
            with ExitStack() as turn:
                if kb:
                    turn.enter_context(nc.sbuf_tensor("before_" + name, [P, int(kb * 256)], F32))
                return turn.enter_context(nc.sbuf_tensor(name, shape, dt))

        ident = sb("ident", [P, P])
        x = sb("x", [P, TOK, D])
        oall = at(0, "oall", [P, 16, VD1])
        p1 = at(16, "p1", [P, 2, 2, SEQ])
        pt1 = at(24, "pt1", [P, 2, SEQ])
        nThi = sb("nThi", [P, KT, SEQ], F32R)
        nTlo = sb("nTlo", [P, KT, SEQ], F32R)
        raw = sb("raw", [P, RING, UNIT])
        whi = sb("whi", [P, RING, UNIT], F32R)
        wlo = sb("wlo", [P, RING, UNIT], F32R)
        gcol = sb("gcol", [P, 2 * LAYERS + 3, KT])
        stat = sb("stat", [P, 3, 4])
        countw = sb("countw", [P, 4, 16])
        lamc = sb("lamc", [P, LAYERS, 2])
        lams = sb("lams", [P, 4])
        sel8 = sb("sel8", [P, 8])
        iw = sb("iw", [P, TOK, 4])
        comb = sb("comb", [P, TOK, EXPERTS])

        M = at(0, "M", [P, TOK, D])
        G = at(16, "G", [P, TOK, D])
        qT = at(32, "qT", [P, 8, SEQ])
        kT = at(48, "kT", [P, 8, SEQ])
        v1 = at(64, "v1", [P, TOK, D])
        qsq = at(16, "qsq", [P, SEQ])
        qy = at(18, "qy", [P, 2, SEQ])
        qrot = at(22, "qrot", [P, 4, 4 * ROT_HALF])
        qst = at(23, "qst", [P, 3, 4])
        win = at(32, "win", [P, 4, SEQ + 16])
        prow = at(41, "prow", [P, D])
        poolhi = at(48, "poolhi", [P, KT, SEQ], F32R)
        poollo = at(64, "poollo", [P, KT, SEQ], F32R)
        qkg = at(80, "qkg", [P, 2, DH1])
        chunkm = at(81, "chunkm", [P, P])
        rope1 = at(81.5, "rope1", [P, TOK, 2 * ROT_HALF])
        subg = at(82, "subg", [P, VD1])
        lvec = at(83, "lvec", [P, 4, DH1])
        qst16 = at(23.5, "qst16", [P, 16])
        ast1 = at(85, "ast1", [P, 10, 16])
        xn = at(0, "xn", [P, TOK, D])
        hf = at(0, "hf", [P, 2, SEQ])
        sg = at(4, "sg", [P, 2, SEQ])
        hhi = at(8, "hhi", [P, 2, SEQ], F32R)
        hlo = at(12, "hlo", [P, 2, SEQ], F32R)
        y2 = at(0, "y2", [P, TOK, 512])
        rot = at(8, "rot", [P, 2, 2, SEQ])
        yThi = at(8, "yThi", [P, 4, SEQ], F32R)
        yTlo = at(16, "yTlo", [P, 4, SEQ], F32R)
        mask2 = at(16, "mask2", [P, SEQ])
        ast2 = at(18, "ast2", [P, 8, 96])
        merged = at(24, "merged", [P, TOK, D])
        gbuf = at(40, "gbuf", [P, TOK, 512])
        p2 = at(76, "p2", [P, 2, SEQ])
        pt2 = at(80, "pt2", [P, 2, SEQ])
        rope2 = at(84, "rope2", [P, TOK, 2 * DH2])
        bq = at(24, "bq", [P, 4, SEQ])
        bk = at(32, "bk", [P, 4, SEQ])
        bv = at(40, "bv", [P, TOK, 512])
        Og = at(48, "Og", [P, 3, TOK * 512])
        score = at(40, "score", [P, 2, SEQ])
        relu = at(44, "relu", [P, 2, SEQ])
        aq = at(48, "aq", [P, 4, SEQ])
        ak = at(56, "ak", [P, 2, SEQ])
        av = at(60, "av", [P, TOK, P])
        iqT = at(62, "iqT", [P, 2, SEQ])
        ik = at(66, "ik", [P, SEQ])
        selb = at(68, "selb", [P, TOK, SEQ])
        memx = at(8, "memx", [P, 2, D])
        memhi = at(48, "memhi", [P, KT, MEM], F32R)
        memlo = at(56, "memlo", [P, KT, MEM], F32R)
        km = at(64, "km", [P, 4, MEM])
        vm = at(68, "vm", [P, 2, 512])
        mqT = at(40, "mqT", [P, 4, SEQ])
        bg = at(72, "bg", [P, 512])
        wr = at(20, "wr", [P, KT, 20])
        wrhi = at(21, "wrhi", [P, KT, 20], F32R)
        wrlo = at(22, "wrlo", [P, KT, 20], F32R)
        rt = at(24, "rt", [P, 16, TOK, 4])
        sl = at(28, "sl", [P, TOK, 20])
        rb = at(29, "rb", [P, 20])
        og = at(16, "og", [P, D])
        memj = at(16, "memj", [P, 2, D])
        sb("arena", [P, 86 * 256])

        bank = [ctx.enter_context(nc.psum_tensor(f"bank{b}", [P, 512], F32)) for b in range(8)]

        raw_full = [sem(f"raw_full{i}") for i in range(RING)]
        hi_done = sem("hi_done")
        split_done = sem("split_done")
        first_half = sem("first_half")
        bank_full = [sem(f"bank_full{b}") for b in range(8)]
        bank_free = [sem(f"bank_free{b}") for b in range(8)]
        s_x = sem("x_landed")
        s_const = sem("const_landed")
        s_layer = sem("layer_rows_landed")
        s_rope2 = sem("rope2_landed")
        s_mask = sem("mask_landed")
        s_bg = sem("bg_landed")
        s_mem = sem("mem_landed")
        s_route = sem("route_landed")
        s_g = sem("final_gain_landed")
        s_store = sem("stored")
        chain = sem("vector_chain")
        sq_done = sem("sq_done")
        ms_done = sem("ms_done")
        root_done = sem("root_done")
        xn_done = sem("xn_done")
        nhi_done = sem("nhi_done")
        mixer_done = sem("mixer_done")
        pooled = sem("pooled")
        poolhi_done = sem("poolhi_done")
        poollo_done = sem("poollo_done")
        qsq_done = sem("qsq_done")
        qms_done = sem("qms_done")
        qroot_done = sem("qroot_done")
        rope_done = sem("rope_done")
        lam_dot = sem("lam_dot")
        lam_exp = sem("lam_exp")
        negmax = sem("negmax")
        mixed = sem("mixed")
        m_done = sem("m_done")
        pad_zero = sem("pad_zero")
        hhi_done = sem("hhi_done")
        hlo_done = sem("hlo_done")
        side_done = sem("side_done")
        relu_used = sem("relu_used")
        exp_done = sem("exp_done")
        y_done = sem("y_done")
        stage = sem("stage")
        bias_used = sem("bias_used")
        sig_done = sem("sig_done")
        shifted = sem("shifted")
        raised = sem("raised")
        wr_hi = sem("wr_hi")
        wr_lo = sem("wr_lo")
        out_done = sem("out_done")

        class Ledger:

            def __init__(self):
                self.unit = 0
                self.split = 0
                self.halves = 0
                self.uses = [0] * 8
                self.released = []
                self.n = {}
                self.x = (s_x, 16)

            def take(self, b):
                self.uses[b] += 1
                return self.uses[b]

            def half(self):
                self.halves += 1
                self.unit += 1
                self.released.append((first_half, self.halves))

            def full(self, b, n):
                self.unit += 1
                self.released.append((bank_full[b], n))

            def tick(self, name, k=1):
                self.n[name] = self.n.get(name, 0) + k
                return self.n[name]

        def cols(w, c0, width=512):
            v = w[:, c0:c0 + width].rearrange("(k p) n -> p k n", p=P)
            for half in range(2):
                yield [(k * width, v[:, 4 * half + k:4 * half + k + 2, :], 2, width) for k in (0, 2)]

        def units_before_groups(l):
            w = A["w_in"][l]
            for c in (0, 1, 8, 9):
                yield from cols(w, c * 512)
            pw = A["pool_w"][l].rearrange("g (k p) n -> p (g k) n", p=P)
            yield [(k * 256, pw[:, k:k + 4, :], 4, 256) for k in (0, 4)]
            for c in (2, 3, 4, 5, 6, 7, 10, 11):
                yield from cols(w, c * 512)
            for c in range(2):
                yield from cols(A["w_out"][l], c * 512)

        def units_second():
            w = A["w_in_2"][0]
            wg = A["w_gate_2"][0]

            def branch(b):
                for half in range(2):
                    yield from cols(wg, b * D + half * 512)
                    v = A["w_branch_2"][0, b].rearrange("(k p) n -> p k n", p=P)[:, :, half * 512:half * 512 + 512]
                    yield [(k * 512, v[:, k:k + 2, :], 2, 512) for k in (0, 2)]

            for g in range(3):
                for c in (BQ, BK, BV):
                    yield from cols(w, c + g * 512)
            yield from branch(1)
            yield from cols(w, AK)
            v = w[:, IK:IK + 68].rearrange("(k p) n -> p k n", p=P)
            yield [(k * 68, v[:, k:k + 4, :], 4, 68) for k in (0, 4)]
            yield from cols(w, AQ)
            yield from branch(0)
            yield from cols(A["w_mem_kv_2"][0], 0)
            yield from cols(A["w_mem_kv_2"][0], 512)
            yield from cols(w, MQ)
            yield from branch(2)
            for c in range(2):
                yield from cols(A["w_out_2"][0], c * 512)

        block = ctx.enter_context(nc.Block())

        @block.sync
        def _(sp):
            c = Ledger()

            def load(s, parts):
                for off, src, k, width in parts:
                    dst = raw[:, s, off:off + k * width].rearrange("p (k n) -> p k n", k=k)
                    sp.dma_start(dst, src).then_inc(raw_full[s], 16)

            def unit(parts):
                if c.unit >= RING:
                    sp.wait_ge(split_done, c.unit - RING + 1)
                load(c.unit % RING, parts)
                c.unit += 1

            def group_in(s0, base, w_gate, w_up):
                for half in range(2):
                    s = (s0 + half) % RING
                    if base is not None:
                        sp.wait_ge(split_done, base + half)
                    for j, w in enumerate((w_gate, w_up)):
                        src = w.rearrange("(k p) n -> p k n", p=P)[:, 4 * half:4 * half + 4, :]
                        dst = raw[:, s, :].rearrange("p (k n) -> p k n", k=4)[:, :, 256 * j:256 * j + 256]
                        sp.dma_start(dst, src).then_inc(raw_full[s], 16)

            def group_out(s, base, w_down):
                sp.wait_ge(split_done, base)
                src = w_down.rearrange("(k p) n -> p k n", p=P)
                for k in (1, 0):
                    sp.dma_start(raw[:, s, k * D:k * D + D], src[:, k, :]).then_inc(raw_full[s], 16)

            sp.dma_start(x[:, :, :], A["x"][0].rearrange("(t p) d -> p t d", p=P)).then_inc(s_x, 16)
            for l in range(LAYERS):
                for parts in units_before_groups(l):
                    unit(parts)
                w1, w2 = A["w_ffn_in"][l], A["w_ffn_out"][l]
                u = c.unit
                group_in(u % RING, u - 2, w1[:, 0:256], w1[:, HID1:HID1 + 256])
                with sp.Fori(0, GROUPS1 - 1) as g:
                    group_in((u + 2) % RING, u + 3 * g,
                             w1[:, bass.ds(256 * g + 256, 256)], w1[:, bass.ds(HID1 + 256 + 256 * g, 256)])
                    group_out((u + 4) % RING, u + 3 * g + 2, w2[bass.ds(256 * g, 256), :])
                group_out((u + 2) % RING, u + 3 * GROUPS1 - 3, w2[HID1 - 256:HID1, :])
                c.unit += 3 * GROUPS1
            for parts in units_second():
                unit(parts)
            w1, w3, w2 = A["w1_2"][0], A["w3_2"][0], A["w2_2"][0]
            u = c.unit
            group_in(u % RING, u - 2, w1[0, :, 0:256], w3[0, :, 0:256])
            with sp.Fori(0, EXPERTS - 1) as e:
                b = u + 6 * e
                group_in((u + 2) % RING, b, w1[e, :, 256:512], w3[e, :, 256:512])
                group_out((u + 4) % RING, b + 2, w2[e, 0:256, :])
                group_in((u + 5) % RING, b + 3, w1[e + 1, :, 0:256], w3[e + 1, :, 0:256])
                group_out((u + 7) % RING, b + 5, w2[e, 256:512, :])
            b = u + 6 * (EXPERTS - 1)
            e = EXPERTS - 1
            group_in((u + 2) % RING, b, w1[e, :, 256:512], w3[e, :, 256:512])
            group_out((u + 4) % RING, b + 2, w2[e, 0:256, :])
            group_out((u + 5) % RING, b + 3, w2[e, 256:512, :])
            for t in range(TOK):
                sp.wait_ge(out_done, t + 1)
                sp.dma_start(out[0, t * P:(t + 1) * P, :], xn[:, t, :]).then_inc(s_store, 16)
            sp.wait_ge(s_store, 16 * TOK)

        @block.gpsimd
        def _(pool):
            def rows(dst, src, s):
                pool.dma_start(dst, src).then_inc(s, 16)

            def gate_bias(b, half):
                c0 = b * D + half * 512
                rows(bg[:, :], A["b_gate_2"][0, c0:c0 + 512].partition_broadcast(P), s_bg)

            rows(ident[:, :], A["c_ident"], s_const)
            rows(gcol[:, :, :], A["c_gains"], s_const)
            rows(chunkm[:, :], A["c_chunk"], s_const)
            rows(rope1[:, :, :], A["c_rope1"], s_const)
            rows(countw[:, :, :], A["c_count"][:, 0:16].partition_broadcast(P), s_const)
            rows(lamc[:, :, :], A["c_lam"].partition_broadcast(P), s_const)
            for l in range(LAYERS):
                if l:
                    pool.wait_ge(mixer_done, l)
                rows(prow[:, :], A["pool_scale"][l].partition_broadcast(P), s_layer)
                rows(qkg[:, 0, :], A["q_norm_g"][l].partition_broadcast(P), s_layer)
                rows(qkg[:, 1, :], A["k_norm_g"][l].partition_broadcast(P), s_layer)
                rows(subg[:, :], A["subln_g"][l].partition_broadcast(P), s_layer)
                for j, name in enumerate(("lam_q1", "lam_k1", "lam_q2", "lam_k2")):
                    rows(lvec[:, j, :], A[name][l].partition_broadcast(P), s_layer)
            pool.wait_ge(mixer_done, LAYERS)
            rows(rope2[:, :, :], A["c_rope2"], s_rope2)
            rows(mask2[:, :], A["c_masks"][0], s_mask)
            gate_bias(1, 0)
            for g in (1, 2):
                pool.wait_ge(stage, g)
                rows(mask2[:, :], A["c_masks"][g], s_mask)
            pool.wait_ge(bias_used, 1)
            gate_bias(1, 1)
            pool.wait_ge(stage, 3)
            rows(mask2[:, :], A["c_masks"][3], s_mask)
            pool.wait_ge(stage, 4)
            gate_bias(0, 0)
            pool.wait_ge(bias_used, 3)
            gate_bias(0, 1)
            pool.wait_ge(stage, 5)
            rows(memx[:, :, :], A["mem_2"][0].rearrange("(t p) d -> p t d", p=P), s_mem)
            gate_bias(2, 0)
            pool.wait_ge(bias_used, 5)
            gate_bias(2, 1)
            pool.wait_ge(stage, 7)
            rows(wr[:, :, 0:4], A["w_group_2"][0].rearrange("(k p) n -> p k n", p=P), s_route)
            for g in range(4):
                rows(wr[:, :, 4 + 4 * g:8 + 4 * g], A["w_sub_2"][0, g].rearrange("(k p) n -> p k n", p=P), s_route)
            rows(rb[:, 0:4], A["b_group_2"][0].partition_broadcast(P), s_route)
            rows(rb[:, 4:20], A["b_sub_2"][0].rearrange("g e -> (g e)").partition_broadcast(P), s_route)
            rows(og[:, :], A["g_final_2"].partition_broadcast(P), s_g)

        def slot_uses(c, tiles=4, halves=2):
            n = [c.take(j) for j in range(tiles)]
            if halves == 2:
                c.half()
            c.full(tiles - 1, n[-1])
            return n

        def groups_begin(c, n):
            before = Before()
            before.unit, before.halves, before.uses, before.n = c.unit, c.halves, list(c.uses), n
            before.h = c.n.get("h", 0)
            return before

        def groups_end(c, w):
            for g in range(w.n):
                c.released.append((first_half, w.halves + g + 1))
                c.released.append((bank_full[3], w.uses[3] + g + 1))
                if g:
                    c.released.append((bank_full[7], w.uses[7] + 2 * g))
            c.released.append((bank_full[7], w.uses[7] + 2 * w.n))
            c.unit += 3 * w.n
            c.halves += w.n
            c.uses = [u + (w.n if b < 4 else 2 * w.n) for b, u in enumerate(c.uses)]
            c.tick("h", w.n)
            c.x = (bank_free[7], c.uses[7])

        class Before:
            pass

        def att_banks(j):
            return j % 4, 4 + j % 2, 6 + j % 2

        ATT1 = [(h, i) for h in range(HEADS1) for i in range(TOK)]
        DIL = [(h, i) for i in range(TOK) for h in range(8)]
        SELA = [(h, i) for i in range(TOK) for h in range(8)]
        MEMA = [(h, i) for i in range(TOK) for h in range(4)]

        def dil_span(g, i):
            if g == 0:
                return max(0, i - 1) * P, min(i + 1, 2) * P
            return 0, (i + 1) * P

        @block.tensor
        def _(pe):
            c = Ledger()

            def take(b):
                n = c.take(b)
                if n > 1:
                    pe.wait_ge(bank_free[b], n - 1)
                return bank[b]

            def product(o, lh, ll, rh, rl, first, last):
                nc.tensor.matmul(o, lh, rh, start=first, stop=False)
                nc.tensor.matmul(o, lh, rl, start=False, stop=False)
                return nc.tensor.matmul(o, ll, rh, start=False, stop=last)

            def wait_unit():
                pe.wait_ge(split_done, c.unit + 1)
                return c.unit % RING

            def wait_left():
                for b in range(4, 8):
                    pe.wait_ge(bank_free[b], c.uses[b])

            def slot(orient, hook=None, left=(nThi, nTlo), tiles=4, n=512, width=512, halves=2):
                lhi, llo = left
                for half in range(halves):
                    s = wait_unit()
                    for j in range(tiles):
                        if half == 0:
                            take(j)
                        nk = 4 if width == 512 else KT
                        for kk in range(nk):
                            k = 4 * half + kk
                            w0 = kk * width
                            if orient == "tok":
                                lt = slice(j * P, j * P + P)
                                last = product(bank[j][:, 0:width], lhi[:, k, lt], llo[:, k, lt],
                                               whi[:, s, w0:w0 + width], wlo[:, s, w0:w0 + width],
                                               half == 0 and kk == 0, half == halves - 1 and kk == nk - 1)
                            else:
                                w0 += j * P
                                last = product(bank[j][:, 0:n], whi[:, s, w0:w0 + P], wlo[:, s, w0:w0 + P],
                                               lhi[:, k, 0:n], llo[:, k, 0:n],
                                               half == 0 and kk == 0, half == halves - 1 and kk == nk - 1)
                        if half == halves - 1:
                            last.then_inc(bank_full[j], 1)
                        elif j == tiles - 1:
                            last.then_inc(first_half, 1)
                        if half == 0 and hook:
                            hook(j)
                    if half == halves - 1:
                        c.full(tiles - 1, c.uses[tiles - 1])
                    else:
                        c.half()

            def to_feature_major(src, tiles, ready, chunks=KT, n0=0):
                for k in range(chunks):
                    b = 4 + k % 4
                    take(b)
                    for t in range(tiles):
                        if k == 0:
                            pe.wait_ge(ready, n0 + t + 1)
                        last = nc.tensor.transpose(bank[b][:, t * P:t * P + P], src[:, t, k * P:k * P + P], ident[:, :])
                    last.then_inc(bank_full[b], 1)

            def head_turns(z, t, views, ready):
                b = 4 + t
                take(b)
                pe.wait_ge(ready, z + 1)
                for j, v in enumerate(views):
                    last = nc.tensor.transpose(bank[b][:, j * P:j * P + P], v, ident[:, :])
                last.then_inc(bank_full[b], 1)

            def groups(n, unroll):
                w = groups_begin(c, n)

                def into(g):
                    for half in range(2):
                        first = w.unit if isinstance(g, int) and g == 0 else w.unit + 3 * g - 1
                        s = (w.unit + half if isinstance(g, int) and g == 0 else into.s + half) % RING
                        pe.wait_ge(split_done, first + half + 1)
                        for j in range(4):
                            if half == 0:
                                pe.wait_ge(bank_free[j], w.uses[j] + g)
                            for kk in range(4):
                                k, w0 = 4 * half + kk, kk * 512 + j * P
                                last = product(bank[j][:, :], whi[:, s, w0:w0 + P], wlo[:, s, w0:w0 + P],
                                               nThi[:, k, :], nTlo[:, k, :], k == 0, k == KT - 1)
                            if half:
                                last.then_inc(bank_full[j], 1)
                        if not half:
                            last.then_inc(first_half, 1)

                def outof(g, unit, s):
                    pe.wait_ge(split_done, unit + 1)
                    pe.wait_ge(hlo_done, w.h + g + 1)
                    for tile in range(8):
                        t, half, b = tile // 2, tile % 2, 4 + tile % 4
                        pe.wait_ge(bank_free[b], w.uses[b] + 2 * g + tile // 4)
                        for kk in range(2):
                            w0 = kk * D + half * 512
                            last = product(bank[b][:, :], hhi[:, kk, t * P:t * P + P], hlo[:, kk, t * P:t * P + P],
                                           whi[:, s, w0:w0 + 512], wlo[:, s, w0:w0 + 512], kk == 0, kk == 1)
                        last.then_inc(bank_full[b], 1)

                into(0)
                with pe.Fori(0, (n - 1) // unroll) as i:
                    for r in range(unroll):
                        g = unroll * i + r
                        into.s = (w.unit + 2) % RING
                        into(g + 1)
                        outof(g, w.unit + 3 * g + 4, (w.unit + 4) % RING)
                for g in range((n - 1) // unroll * unroll, n - 1):
                    into(g + 1)
                    outof(g, w.unit + 3 * g + 4, (w.unit + 4) % RING)
                outof(n - 1, w.unit + 3 * n - 1, (w.unit + 3 * n - 1) % RING)
                groups_end(c, w)

            pe.wait_ge(s_const, 16 * 6)
            for l in range(LAYERS):
                to_feature_major(xn, TOK, xn_done, n0=c.n.get("xn", 0))
                c.tick("xn", TOK)
                wait_left()
                slot("feat")
                slot("feat")
                slot("tok")
                slot("tok")
                s = wait_unit()
                pe.wait_ge(poollo_done, KT * (l + 1))
                for t in range(TOK):
                    for gp in range(2):
                        b = 4 + (2 * t + gp) % 4
                        take(b)
                        for g in (2 * gp, 2 * gp + 1):
                            o = bank[b][:, (g % 2) * 256:(g % 2) * 256 + 256]
                            for kk in range(2):
                                k, w0 = 2 * g + kk, (2 * g + kk) * 256
                                last = product(o, poolhi[:, k, t * P:t * P + P], poollo[:, k, t * P:t * P + P],
                                               whi[:, s, w0:w0 + 256], wlo[:, s, w0:w0 + 256], kk == 0, kk == 1)
                        last.then_inc(bank_full[b], 1)
                c.full(7, c.uses[7])

                def qk_turns(i):
                    def hook(t):
                        z = 4 * i + t
                        v = qy[:, z % 2, :]
                        head_turns(c.n.get("rope", 0) + z, t, [v[:, j * P:j * P + P] for j in range(4)], rope_done)
                    return hook

                slot("tok")
                slot("tok", qk_turns(0))
                slot("tok", qk_turns(1))
                slot("tok", qk_turns(2))
                slot("tok", qk_turns(3))
                slot("tok")
                c.tick("rope", 16)
                slot("tok")
                slot("tok")

                def logits(j):
                    h, i = ATT1[j]
                    w = (i + 1) * P
                    for comp in range(2):
                        b = 2 * (j % 2) + comp
                        take(b)
                        hc = 2 * h + comp
                        nc.tensor.matmul(bank[b][:, 0:w], qT[:, hc, i * P:i * P + P], kT[:, hc, 0:w],
                                         start=True, stop=False)
                        nc.tensor.matmul(bank[b][:, w - P:w], ident[:, :], chunkm[:, :],
                                         start=False, stop=True).then_inc(bank_full[b], 1)

                def turn(j):
                    h, i = ATT1[j]
                    b = 4 + j % 2
                    take(b)
                    pe.wait_ge(mixed, c.n.get("mixed", 0) + j + 1)
                    for kb in range(i + 1):
                        last = nc.tensor.transpose(bank[b][:, kb * P:kb * P + P], p1[:, j % 2, 0, kb * P:kb * P + P],
                                                   ident[:, :])
                    last.then_inc(bank_full[b], 1)

                def values(j):
                    h, i = ATT1[j]
                    b = 6 + j % 2
                    take(b)
                    tb = 4 + j % 2
                    pe.wait_ge(bank_free[tb], c.uses[tb])
                    for kb in range(i + 1):
                        last = nc.tensor.matmul(bank[b][:, 0:VD1], pt1[:, j % 2, kb * P:kb * P + P],
                                                v1[:, kb, h * VD1:h * VD1 + VD1], start=kb == 0, stop=kb == i)
                    last.then_inc(bank_full[b], 1)

                for b in range(8):
                    pe.wait_ge(bank_free[b], c.uses[b])
                logits(0)
                logits(1)
                for j in range(len(ATT1)):
                    turn(j)
                    if j:
                        values(j - 1)
                    if j + 2 < len(ATT1):
                        logits(j + 2)
                values(j)
                c.tick("mixed", len(ATT1))

                to_feature_major(M, TOK, m_done, n0=TOK * l)
                wait_left()
                slot("tok")
                slot("tok")

                to_feature_major(xn, TOK, xn_done, n0=c.n["xn"])
                c.tick("xn", TOK)
                wait_left()
                groups(GROUPS1, 1)

            to_feature_major(xn, TOK, xn_done, n0=c.n["xn"])
            c.tick("xn", TOK)
            wait_left()

            def pair_turns(a, pairs):
                def hook(t):
                    v = rot[:, t % 2, 0, :]
                    head_turns(a + t, t, [pairs(v, j) for j in range(4)], rope_done)
                return hook

            def plain_pair(v, j):
                return v[:, j * P:j * P + P]

            def indexer_turns(a):
                return lambda t: head_turns(a + t, t, [rot[:, t % 2, int(j < 2), j * P:j * P + P] for j in range(4)],
                                            rope_done)

            def attention(items, q, k, v, span, vw, maxed):
                def logits(j):
                    h, i = items[j]
                    b = j % 4
                    take(b)
                    k0, w = span(i)
                    nc.tensor.matmul(bank[b][:, 0:w], q(h, i), k(h, k0, w), start=True, stop=True)\
                        .then_inc(bank_full[b], 1)

                def turn(j):
                    h, i = items[j]
                    b = 4 + j % 2
                    take(b)
                    pe.wait_ge(exp_done, maxed + j + 1)
                    k0, w = span(i)
                    for kb in range(w // P):
                        last = nc.tensor.transpose(bank[b][:, kb * P:kb * P + P], p2[:, j % 2, kb * P:kb * P + P],
                                                   ident[:, :])
                    last.then_inc(bank_full[b], 1)

                def values(j):
                    h, i = items[j]
                    b = 6 + j % 2
                    take(b)
                    tb = 4 + j % 2
                    pe.wait_ge(bank_free[tb], c.uses[tb])
                    k0, w = span(i)
                    for kb in range(w // P):
                        last = nc.tensor.matmul(bank[b][:, 0:vw], pt2[:, j % 2, kb * P:kb * P + P],
                                                v(h, k0 // P + kb), start=kb == 0, stop=kb == w // P - 1)
                    last.then_inc(bank_full[b], 1)

                for b in range(8):
                    pe.wait_ge(bank_free[b], c.uses[b])
                logits(0)
                logits(1)
                for j in range(len(items)):
                    turn(j)
                    if j:
                        values(j - 1)
                    if j + 2 < len(items):
                        logits(j + 2)
                values(j)

            def lane(t, h, j, c0, w):
                r = DH2 * (h % 2)
                return t[r:r + DH2, j, c0:c0 + w]

            def merge(b):
                to_feature_major(y2, TOK, y_done, chunks=4, n0=c.n.get("y", 0))
                c.tick("y", TOK)
                wait_left()
                for half in range(2):
                    slot("tok")
                    slot("tok", left=(yThi, yTlo), halves=1)

            for g in range(3):
                a = c.n["rope"]
                slot("tok")
                slot("tok", pair_turns(a, plain_pair))
                slot("tok", pair_turns(a + TOK, plain_pair))
                c.tick("rope", 2 * TOK)
                attention(DIL, lambda h, i: lane(bq, h, h // 2, i * P, P), lambda h, k0, w: lane(bk, h, h // 2, k0, w),
                          lambda h, kb: bv[:, kb, h * DH2:h * DH2 + DH2], lambda i: dil_span(g, i), DH2,
                          c.n.get("exp", 0))
                c.tick("exp", len(DIL))
            merge(1)

            a = c.n["rope"]
            slot("tok")
            slot("tok", indexer_turns(a), width=68, halves=1)

            def ik_turns(t):
                head_turns(a + TOK + t, t, [rot[:, t % 2, 1, 0:P]], rope_done)

            slot("tok", ik_turns)
            for t in range(TOK):
                pair_turns(a + 2 * TOK, plain_pair)(t)
            c.tick("rope", 3 * TOK)
            for b in range(8):
                pe.wait_ge(bank_free[b], c.uses[b])
            for i in range(1, TOK):
                for h in range(4):
                    take(h)
                    nc.tensor.matmul(bank[h][:, 0:(i + 1) * P], lane(iqT, h, h // 2, i * P, P),
                                     ik[DH2 * (h % 2):DH2 * (h % 2) + DH2, 0:(i + 1) * P], start=True, stop=True)\
                        .then_inc(bank_full[h], 1)
            attention(SELA, lambda h, i: lane(aq, h, h // 2, i * P, P), lambda h, k0, w: lane(ak, h, h // 4, k0, w),
                      lambda h, kb: av[:, kb, (h // 4) * DH2:(h // 4) * DH2 + DH2], lambda i: (0, (i + 1) * P), DH2,
                      c.n["exp"])
            c.tick("exp", len(SELA))
            merge(0)

            for k in range(KT):
                b = 4 + k % 4
                take(b)
                for t in range(2):
                    if k == 0:
                        pe.wait_ge(xn_done, c.n["xn"] + t + 1)
                    last = nc.tensor.transpose(bank[b][:, t * P:t * P + P], memx[:, t, k * P:k * P + P], ident[:, :])
                last.then_inc(bank_full[b], 1)
            c.tick("xn", 2)
            wait_left()
            slot("feat", left=(memhi, memlo), n=MEM)
            slot("tok", left=(memhi, memlo), tiles=2)
            slot("feat")
            attention(MEMA, lambda h, i: mqT[:, h, i * P:i * P + P], lambda h, k0, w: km[:, h, k0:k0 + w],
                      lambda h, kb: vm[:, kb, h * P:h * P + P], lambda i: (0, MEM), P, c.n["exp"])
            c.tick("exp", len(MEMA))
            merge(2)

            pe.wait_ge(stage, 6)
            for k in range(KT):
                b = 4 + k % 4
                take(b)
                for t in range(TOK):
                    last = nc.tensor.transpose(bank[b][:, t * P:t * P + P], merged[:, t, k * P:k * P + P], ident[:, :])
                last.then_inc(bank_full[b], 1)
            wait_left()
            slot("tok")
            slot("tok")

            to_feature_major(xn, TOK, xn_done, n0=c.n["xn"])
            wait_left()
            pe.wait_ge(wr_lo, 1)
            for t in range(TOK):
                take(t)
                for k in range(KT):
                    last = product(bank[t][:, 0:20], nThi[:, k, t * P:t * P + P], nTlo[:, k, t * P:t * P + P],
                                   wrhi[:, k, :], wrlo[:, k, :], k == 0, k == KT - 1)
                last.then_inc(bank_full[t], 1)
            groups(GROUPS2, 2)

        @block.scalar
        def _(act):
            c = Ledger()

            def hi_part(s, width=UNIT):
                return nc.scalar.activation(whi[:, s, 0:width], raw[:, s, 0:width], ACT.Copy)

            def split_to(u):
                while c.split < min(u, TOTAL_UNITS):
                    v = c.split
                    act.wait_ge(raw_full[v % RING], 32 * (v // RING + 1))
                    if v >= RING:
                        act.wait_ge(*c.released[v - RING])
                    hi_part(v % RING, 8 * 68 if v == NARROW_UNIT else UNIT).then_inc(hi_done, 1)
                    c.split += 1

            def norm_roots(src, tiles, junk):
                for t in range(tiles):
                    nc.scalar.activation(junk(t), src[:, t, :], ACT.Square, accum_out=stat[:, 0, t:t + 1])\
                        .then_inc(sq_done, 1)
                act.wait_ge(ms_done, c.tick("ms"))
                nc.scalar.activation(stat[:, 0, 0:tiles], stat[:, 1, 0:tiles], ACT.Sqrt).then_inc(root_done, 1)

            def left_hi(hi, gain=None, chunks=KT, n=SEQ):
                for k in range(chunks):
                    b = 4 + k % 4
                    act.wait_ge(bank_full[b], c.take(b))
                    if gain is None:
                        ins = nc.scalar.activation(hi[:, k, 0:n], bank[b][:, 0:n], ACT.Copy)
                    else:
                        ins = nc.scalar.activation(hi[:, k, 0:n], bank[b][:, 0:n], ACT.Identity,
                                                   scale=gcol[:, gain, k:k + 1])
                    ins.then_inc(nhi_done, 1)

            def norm(gain):
                act.wait_ge(*c.x)
                norm_roots(x, TOK, lambda t: xn[:, t, :])
                left_hi(nThi, gain)

            def evacuate(outs, func=ACT.Copy, tiles=4, halves=2, n=512, **more):
                uses = slot_uses(c, tiles, halves)
                split_to(c.unit + 2)
                for j in range(tiles):
                    act.wait_ge(bank_full[j], uses[j])
                    nc.scalar.activation(outs(j), bank[j][:, 0:n], func, **more).then_inc(bank_free[j], 1)
                split_to(c.unit + 3)

            def turned(outs):
                for t in range(TOK):
                    b = 4 + t
                    act.wait_ge(bank_full[b], c.take(b))
                    for dst, c0, w in outs(t):
                        ins = nc.scalar.activation(dst, bank[b][:, c0:c0 + w].rearrange("p (j n) -> p j n", n=P),
                                                   ACT.Copy)
                    ins.then_inc(bank_free[b], 1)

            def groups(n, unroll):
                w = groups_begin(c, n)

                def silu(g):
                    for j in range(2):
                        act.wait_ge(bank_full[j], w.uses[j] + g + 1)
                        act.wait_ge(bank_free[2 + j], w.uses[2 + j] + g)
                        nc.scalar.activation(sg[:, j, :], bank[j][:, :], ACT.Silu).then_inc(bank_free[j], 1)

                def hidden_hi(g):
                    act.wait_ge(bank_free[3], w.uses[3] + g + 1)
                    act.wait_ge(bank_full[7], w.uses[7] + 2 * g)
                    nc.scalar.activation(hhi[:, :, :], hf[:, :, :], ACT.Copy).then_inc(hhi_done, 1)

                def split_unit(u, s, turns, released):
                    act.wait_ge(raw_full[s], turns)
                    act.wait_ge(*released)
                    hi_part(s).then_inc(hi_done, 1)

                c.half()
                c.full(3, w.uses[3] + 1)
                split_to(w.unit + 4)
                silu(0)
                split_to(w.unit + 5)
                hidden_hi(0)

                def landed(r, g):
                    return 32 * ((w.unit + r) // RING + 1) + 32 * g

                def body(g):
                    s = [(w.unit + r) % RING for r in (5, 6, 7)]
                    split_unit(5, s[0], landed(5, g), (first_half, w.halves + g + 2))
                    silu(g + 1)
                    split_unit(6, s[1], landed(6, g), (bank_full[3], w.uses[3] + g + 2))
                    split_unit(7, s[2], landed(7, g), (bank_full[7], w.uses[7] + 2 * g + 2))
                    hidden_hi(g + 1)

                with act.Fori(0, (n - 1) // unroll) as i:
                    for r in range(unroll):
                        body(unroll * i + r)
                done = (n - 1) // unroll * unroll
                for g in range(done, n - 1):
                    s = (w.unit + 3 * n - 1) % RING
                    split_unit(5, s, landed(5, g), (first_half, w.halves + g + 2))
                    silu(g + 1)
                    hidden_hi(g + 1)
                c.halves, c.unit, c.released[w.unit:] = w.halves, w.unit, []
                groups_end(c, w)
                c.split = min(w.unit + 3 * n + 2, TOTAL_UNITS)

            act.wait_ge(s_const, 16 * 6)
            for l in range(LAYERS):
                norm(2 * l)
                for _ in range(2):
                    uses = slot_uses(c)
                    split_to(c.unit + 2)
                    for j in range(4):
                        m = c.tick("u")
                        act.wait_ge(bank_full[j], uses[j])
                        if m == 1 or (m - 1) % KT == 0:
                            act.wait_ge(pad_zero, l + 1)
                        nc.scalar.activation(win[:, m % 2, 16:16 + SEQ], bank[j][:, :], ACT.Copy)\
                            .then_inc(bank_free[j], 1)
                        act.wait_ge(pooled, m)
                        nc.scalar.activation(poolhi[:, (m - 1) % KT, :], win[:, 2, 16:16 + SEQ], ACT.Copy)\
                            .then_inc(poolhi_done, 1)
                    split_to(c.unit + 3)
                for half in range(2):
                    evacuate(lambda j: M[:, j, half * 512:half * 512 + 512], ACT.Sigmoid)
                for k in range(8):
                    c.take(4 + k % 4)
                c.full(7, c.uses[7])
                for i in range(4):
                    uses = slot_uses(c)
                    split_to(c.unit + 2)
                    for t in range(TOK):
                        z = c.tick("qk")
                        act.wait_ge(bank_full[t], uses[t])
                        if z > 1:
                            act.wait_ge(qms_done, z - 1)
                        nc.scalar.activation(qsq[:, :], bank[t][:, :], ACT.Square).then_inc(qsq_done, 1)
                        act.wait_ge(qms_done, z)
                        nc.scalar.activation(qst[:, 0, :], qst[:, 1, :], ACT.Sqrt).then_inc(qroot_done, 1)
                    split_to(c.unit + 3)
                    dst = (qT, kT)[i // 2]
                    turned(lambda t: [(dst[:, 4 * (i % 2):4 * (i % 2) + 4, t * P:t * P + P], 0, 512)])
                for half in range(2):
                    evacuate(lambda j: v1[:, j, half * 512:half * 512 + 512])
                for half in range(2):
                    evacuate(lambda j: G[:, j, half * 512:half * 512 + 512], ACT.Sigmoid)
                act.wait_ge(lam_dot, l + 1)
                nc.scalar.activation(lams[:, 2:4], lams[:, 0:2], ACT.Exp).then_inc(lam_exp, 1)

                j0 = c.n.get("neg", 0)
                uses = []
                for j in range(len(ATT1)):
                    bs = (2 * (j % 2), 2 * (j % 2) + 1, 4 + j % 2, 6 + j % 2)
                    uses.append([(b, c.take(b)) for b in bs])

                def exps(j):
                    h, i = ATT1[j]
                    w = (i + 1) * P
                    act.wait_ge(negmax, j0 + j + 1)
                    for comp in range(2):
                        b, n = uses[j][comp]
                        if j >= 2:
                            tb, tn = uses[j - 2][2]
                            act.wait_ge(bank_full[tb], tn)
                        nc.scalar.activation(p1[:, j % 2, comp, 0:w], bank[b][:, 0:w], ACT.Exp, scale=SCALE1,
                                             bias=ast1[:, 2 + comp, j:j + 1], accum_out=ast1[:, 4 + comp, j:j + 1])\
                            .then_inc(bank_free[b], 1)

                def turned_weights(j):
                    w = (ATT1[j][1] + 1) * P
                    b, n = uses[j][2]
                    act.wait_ge(bank_full[b], n)
                    if j >= 2:
                        act.wait_ge(bank_full[uses[j - 2][3][0]], uses[j - 2][3][1])
                    nc.scalar.activation(pt1[:, j % 2, 0:w], bank[b][:, 0:w], ACT.Copy).then_inc(bank_free[b], 1)

                def result(j):
                    b, n = uses[j][3]
                    act.wait_ge(bank_full[b], n)
                    if j >= 2:
                        act.wait_ge(bank_free[b], n - 1)
                    nc.scalar.activation(lvec[:, 2 * (j % 2):2 * (j % 2) + 2, :].rearrange("p a b -> p (a b)"), bank[b][:, 0:VD1], ACT.Square,
                                         scale=ast1[:, 6, j:j + 1], accum_out=ast1[:, 7, j:j + 1])
                    nc.scalar.activation(oall[:, j, :], bank[b][:, 0:VD1], ACT.Identity, scale=ast1[:, 6, j:j + 1])\
                        .then_inc(bank_free[b], 1)

                for j in range(len(ATT1) + 2):
                    if j < len(ATT1):
                        exps(j)
                    if 1 <= j <= len(ATT1):
                        turned_weights(j - 1)
                    if j >= 2:
                        result(j - 2)
                c.tick("neg", len(ATT1))
                act.wait_ge(ms_done, c.tick("ms"))
                nc.scalar.activation(ast1[:, 8, :], ast1[:, 7, :], ACT.Sqrt).then_inc(root_done, 1)

                left_hi(nThi)
                slot_uses(c)
                split_to(c.unit + 3)
                uses = slot_uses(c)
                split_to(c.unit + 3)
                c.x = (bank_free[3], uses[3])
                norm(2 * l + 1)
                groups(GROUPS1, 1)

            norm(2 * LAYERS)

            def attention(items, span, vw, outs, masked, scale):
                uses = []
                e0 = c.n.get("exp", 0)
                for j in range(len(items)):
                    uses.append([(b, c.take(b)) for b in (j % 4, 4 + j % 2, 6 + j % 2)])

                def exps(j):
                    w = span(items[j][1])[1]
                    act.wait_ge(negmax, c.n["neg"] + j + 1)
                    src = p2[:, j % 2, 0:w] if masked else bank[j % 4][:, 0:w]
                    if not masked and j >= 2:
                        act.wait_ge(bank_full[uses[j - 2][1][0]], uses[j - 2][1][1])
                    nc.scalar.activation(p2[:, j % 2, 0:w], src, ACT.Exp, scale=scale,
                                         bias=ast2[:, 1, outs(j):outs(j) + 1],
                                         accum_out=ast2[:, 2, outs(j):outs(j) + 1]).then_inc(exp_done, 1)

                def turned_weights(j):
                    w = span(items[j][1])[1]
                    b, n = uses[j][1]
                    act.wait_ge(bank_full[b], n)
                    if j >= 2:
                        act.wait_ge(bank_full[uses[j - 2][2][0]], uses[j - 2][2][1])
                    nc.scalar.activation(pt2[:, j % 2, 0:w], bank[b][:, 0:w], ACT.Copy).then_inc(bank_free[b], 1)

                for j in range(len(items) + 1):
                    if j < len(items):
                        exps(j)
                    if j:
                        turned_weights(j - 1)
                c.tick("neg", len(items))
                c.tick("exp", len(items))

            def merge(b):
                left_hi(yThi, chunks=4)
                for half in range(2):
                    slot_uses(c)
                    split_to(c.unit + 2)
                    for t in range(TOK):
                        act.wait_ge(bank_free[t], c.uses[t])
                        nc.scalar.activation(gbuf[:, t, :], gbuf[:, t, :], ACT.Sigmoid).then_inc(sig_done, 1)
                    split_to(c.unit + 3)
                    slot_uses(c, halves=1)
                    split_to(c.unit + 2)

            def pairs_to(dst):
                turned(lambda t: [(dst[:, :, t * P:t * P + P], 0, 512)])

            for g in range(3):
                for dst in (bq, bk):
                    slot_uses(c)
                    split_to(c.unit + 3)
                    pairs_to(dst)
                evacuate(lambda j: bv[:, j, :])
                attention(DIL, lambda i: dil_span(g, i), DH2,
                          lambda j: g * 32 + DIL[j][1] * 8 + DIL[j][0], True, SCALE2)
            act.wait_ge(shifted, 1)
            nc.scalar.activation(ast2[:, 4, :], ast2[:, 3, :], ACT.Exp, scale=SCALE2).then_inc(raised, 1)
            merge(1)

            uses = slot_uses(c)
            split_to(c.unit + 2)
            for t in range(TOK):
                act.wait_ge(bank_full[t], uses[t])
                nc.scalar.activation(av[:, t, :], bank[t][:, 128:256], ACT.Copy).then_inc(side_done, 1)
            split_to(c.unit + 3)
            turned(lambda t: [(ak[:, :, t * P:t * P + P], 0, 256), (iqT[:, :, t * P:t * P + P], 256, 256)])
            uses = slot_uses(c, halves=1)
            split_to(c.unit + 2)
            for t in range(TOK):
                act.wait_ge(bank_full[t], uses[t])
                nc.scalar.activation(iw[:, t, :], bank[t][:, 64:68], ACT.Copy, scale=0.5).then_inc(side_done, 1)
            split_to(c.unit + 3)
            turned(lambda t: [(ik[:, t * P:t * P + P].unsqueeze(1), 0, 128)])
            slot_uses(c)
            split_to(c.unit + 3)
            pairs_to(aq)
            n = 0
            for i in range(1, TOK):
                for h in range(4):
                    act.wait_ge(bank_full[h], c.take(h))
                    if n >= 2:
                        act.wait_ge(relu_used, n - 1)
                    nc.scalar.activation(relu[:, h % 2, 0:(i + 1) * P], bank[h][:, 0:(i + 1) * P], ACT.Relu,
                                         scale=0.125).then_inc(bank_free[h], 1)
                    n += 1
            attention(SELA, lambda i: (0, (i + 1) * P), DH2, lambda j: j, True, SCALE2)
            merge(0)

            act.wait_ge(s_mem, 16)
            norm_roots(memx, 2, lambda t: memj[:, t, :])
            left_hi(memhi, 2 * LAYERS + 2, n=MEM)
            evacuate(lambda j: km[:, j, :], n=MEM)
            evacuate(lambda j: vm[:, j, :], tiles=2)
            evacuate(lambda j: mqT[:, j, :])
            attention(MEMA, lambda i: (0, MEM), P, lambda j: j, False, SCALE_M)
            merge(2)
            left_hi(nThi)
            slot_uses(c)
            split_to(c.unit + 3)
            uses = slot_uses(c)
            split_to(c.unit + 3)
            c.x = (bank_free[3], uses[3])

            norm(2 * LAYERS + 1)
            act.wait_ge(s_route, 16 * 7)
            nc.scalar.activation(wrhi[:, :, :], wr[:, :, :], ACT.Copy).then_inc(wr_hi, 1)
            for t in range(TOK):
                c.take(t)
            act.wait_ge(shifted, 2)
            nc.scalar.activation(rt[:, 1, :, :], rt[:, 0, :, :], ACT.Exp).then_inc(raised, 1)
            act.wait_ge(shifted, 3)
            nc.scalar.activation(rt[:, 9, :, 0:1], rt[:, 8, :, 0:1], ACT.Exp).then_inc(raised, 1)
            groups(GROUPS2, 2)

            act.wait_ge(*c.x)
            norm_roots(x, TOK, lambda t: xn[:, t, :])

        @block.vector
        def _(dve):
            c = Ledger()
            v = nc.vector

            def note(ins):
                ins.then_inc(chain, c.tick("chain") and 1)

            def settle():
                dve.wait_ge(chain, c.n["chain"])

            def link(ins):
                note(ins)
                settle()

            def lo_part(s, width=UNIT):
                return v.tensor_tensor(wlo[:, s, 0:width], raw[:, s, 0:width], whi[:, s, 0:width].bitcast(F32),
                                       ALU.subtract)

            def split_to(u):
                while c.split < min(u, TOTAL_UNITS):
                    w = c.split
                    dve.wait_ge(hi_done, w + 1)
                    lo_part(w % RING, 8 * 68 if w == NARROW_UNIT else UNIT).then_inc(split_done, 1)
                    c.split += 1

            def mean_roots(tiles, width):
                dve.wait_ge(sq_done, c.tick("sq", tiles))
                v.tensor_scalar(stat[:, 1, 0:tiles], stat[:, 0, 0:tiles], 1.0 / width, EPS, ALU.mult, ALU.add)\
                    .then_inc(ms_done, 1)
                dve.wait_ge(root_done, c.tick("root"))
                link(v.reciprocal(stat[:, 2, 0:tiles], stat[:, 0, 0:tiles]))

            def left_lo(hi, lo, gain=None, chunks=KT, n=SEQ):
                for k in range(chunks):
                    b = 4 + k % 4
                    c.take(b)
                    dve.wait_ge(nhi_done, c.tick("nhi"))
                    top = hi[:, k, 0:n].bitcast(F32)
                    if gain is None:
                        ins = v.tensor_tensor(lo[:, k, 0:n], bank[b][:, 0:n], top, ALU.subtract)
                    else:
                        ins = v.scalar_tensor_tensor(out=lo[:, k, 0:n], in0=bank[b][:, 0:n],
                                                     scalar=gcol[:, gain, k:k + 1], in1=top,
                                                     op0=ALU.mult, op1=ALU.subtract)
                    ins.then_inc(bank_free[b], 1)

            def norm(gain):
                mean_roots(TOK, D)
                for t in range(TOK):
                    v.tensor_scalar(xn[:, t, :], x[:, t, :], stat[:, 2, t:t + 1], None, ALU.mult).then_inc(xn_done, 1)
                left_lo(nThi, nTlo, gain)

            def add_to_x(half):
                uses = slot_uses(c)
                split_to(c.unit + 2)
                for t in range(TOK):
                    dve.wait_ge(bank_full[t], uses[t])
                    xs = x[:, t, half * 512:half * 512 + 512]
                    v.tensor_tensor(xs, bank[t][:, :], xs, ALU.add).then_inc(bank_free[t], 1)
                split_to(c.unit + 3)
                c.x = (bank_free[3], uses[3])

            def groups(n, unroll, weight=None):
                w = groups_begin(c, n)

                def hidden(g):
                    for j in range(2):
                        dve.wait_ge(bank_free[j], w.uses[j] + g + 1)
                        dve.wait_ge(bank_full[2 + j], w.uses[2 + j] + g + 1)
                        if j == 0:
                            dve.wait_ge(hlo_done, w.h + g) if not (isinstance(g, int) and w.h + g < 1) else None
                        v.tensor_tensor(hf[:, j, :], bank[2 + j][:, :], sg[:, j, :], ALU.mult)\
                            .then_inc(bank_free[2 + j], 1)

                def hidden_lo(g):
                    dve.wait_ge(hhi_done, w.h + g + 1)
                    v.tensor_tensor(hlo[:, :, :], hf[:, :, :], hhi[:, :, :].bitcast(F32), ALU.subtract)\
                        .then_inc(hlo_done, 1)

                def outof(g, e):
                    dve.wait_ge(bank_free[7], w.uses[7] + 2 * g)
                    for tile in range(8):
                        t, half, b = tile // 2, tile % 2, 4 + tile % 4
                        dve.wait_ge(bank_full[b], w.uses[b] + 2 * g + tile // 4 + 1)
                        xs = x[:, t, half * 512:half * 512 + 512]
                        if weight is None:
                            ins = v.tensor_tensor(xs, bank[b][:, :], xs, ALU.add)
                        else:
                            ins = v.scalar_tensor_tensor(out=xs, in0=bank[b][:, :], scalar=weight(t, e), in1=xs,
                                                         op0=ALU.mult, op1=ALU.add)
                        ins.then_inc(bank_free[b], 1)

                def split_unit(r, g):
                    u = w.unit + r + 3 * g
                    dve.wait_ge(hi_done, u + 1)
                    lo_part((w.unit + r) % RING).then_inc(split_done, 1)

                c.half()
                c.full(3, w.uses[3] + 1)
                split_to(w.unit + 4)
                hidden(0)
                split_to(w.unit + 5)
                hidden_lo(0)
                with dve.Fori(0, (n - 1) // unroll) as i:
                    for r in range(unroll):
                        g = unroll * i + r
                        split_unit(5, g)
                        hidden(g + 1)
                        split_unit(6, g)
                        outof(g, i)
                        split_unit(7, g)
                        hidden_lo(g + 1)
                done = (n - 1) // unroll * unroll
                for g in range(done, n - 1):
                    split_unit(5, g)
                    hidden(g + 1)
                    outof(g, g // unroll)
                    hidden_lo(g + 1)
                outof(n - 1, (n - 1) // unroll)
                c.halves, c.unit, c.released[w.unit:] = w.halves, w.unit, []
                groups_end(c, w)
                c.split = min(w.unit + 3 * n + 2, TOTAL_UNITS)

            dve.wait_ge(s_const, 16 * 6)
            dve.wait_ge(*c.x)
            for l in range(LAYERS):
                norm(2 * l)
                v.memset(win[:, :, 0:16], 0.0).then_inc(pad_zero, 1)
                dve.wait_ge(pad_zero, l + 1)
                for _ in range(2):
                    uses = slot_uses(c)
                    split_to(c.unit + 2)
                    for j in range(4):
                        m = c.tick("u")
                        g = (m - 1) % KT // 2
                        dve.wait_ge(bank_free[j], uses[j])
                        here, at_ = win[:, m % 2, :], 3
                        for level in range(g + 1):
                            link(v.tensor_tensor(win[:, at_, 16:16 + SEQ], here[:, 16:16 + SEQ],
                                                 here[:, 16 - 2 ** level:16 + SEQ - 2 ** level], ALU.add))
                            here, at_ = win[:, at_, :], 5 - at_
                        u = win[:, m % 2, :]
                        link(v.tensor_tensor(qst16[:, :], here[:, 16:32], countw[:, g, :], ALU.mult))
                        link(v.scalar_tensor_tensor(out=win[:, 2, 32:16 + SEQ], in0=here[:, 32:16 + SEQ],
                                                    scalar=1.0 / POOL_WINDOWS[g], in1=u[:, 32:16 + SEQ],
                                                    op0=ALU.mult, op1=ALU.subtract))
                        v.tensor_tensor(win[:, 2, 16:32], qst16[:, :], u[:, 16:32], ALU.subtract).then_inc(pooled, 1)
                        dve.wait_ge(poolhi_done, m)
                        v.tensor_tensor(poollo[:, (m - 1) % KT, :], win[:, 2, 16:16 + SEQ],
                                        poolhi[:, (m - 1) % KT, :].bitcast(F32), ALU.subtract).then_inc(poollo_done, 1)
                        dve.wait_ge(poollo_done, m)
                    split_to(c.unit + 3)
                dve.wait_ge(s_layer, 16 * 8 * (l + 1))
                for half in range(2):
                    uses = slot_uses(c)
                    split_to(c.unit + 2)
                    for t in range(TOK):
                        dve.wait_ge(bank_free[t], uses[t])
                        ms = M[:, t, half * 512:half * 512 + 512]
                        note(v.tensor_tensor(ms, ms, prow[:, half * 512:half * 512 + 512], ALU.mult))
                    split_to(c.unit + 3)
                settle()
                for k in range(8):
                    b = 4 + k % 4
                    dve.wait_ge(bank_full[b], c.take(b))
                    ms = M[:, k // 2, (k % 2) * 512:(k % 2) * 512 + 512]
                    v.tensor_tensor(ms, bank[b][:, :], ms, ALU.mult).then_inc(bank_free[b], 1)
                c.full(7, c.uses[7])

                zs = []
                for i in range(4):
                    uses = slot_uses(c)
                    split_to(c.unit + 2)
                    for t in range(TOK):
                        z = c.tick("qk")
                        y = qy[:, (z - 1) % 2, :].rearrange("p (j n) -> p j n", n=P)
                        dve.wait_ge(qsq_done, z)
                        link(v.tensor_reduce(qst[:, 2, :], qsq[:, :].rearrange("p (j n) -> p j n", n=P), AX.X, ALU.add))
                        v.tensor_scalar(qst[:, 1, :], qst[:, 2, :], 1.0 / DH1, EPS, ALU.mult, ALU.add)\
                            .then_inc(qms_done, 1)
                        dve.wait_ge(qroot_done, z)
                        link(v.reciprocal(qst[:, 2, :], qst[:, 0, :]))
                        if len(zs) >= 2:
                            dve.wait_ge(*zs[-2])
                        for j in range(4):
                            ins = v.scalar_tensor_tensor(out=y[:, j, :], in0=bank[t][:, j * P:j * P + P],
                                                         scalar=qst[:, 2, j:j + 1], in1=qkg[:, i // 2, :],
                                                         op0=ALU.mult, op1=ALU.mult)
                            if j < 3:
                                note(ins)
                        ins.then_inc(bank_free[t], 1)
                        dve.wait_ge(bank_free[t], uses[t])
                        cos = rope1[:, t, 0:ROT_HALF].unsqueeze(1).to_broadcast([P, 4, ROT_HALF])
                        sin = rope1[:, t, ROT_HALF:2 * ROT_HALF].unsqueeze(1).to_broadcast([P, 4, ROT_HALF])
                        y1, y2_ = y[:, :, 0:ROT_HALF], y[:, :, ROT_HALF:2 * ROT_HALF]
                        r = [qrot[:, k, :].rearrange("p (j n) -> p j n", n=ROT_HALF) for k in range(4)]
                        note(v.tensor_tensor(r[0], y1, cos, ALU.mult))
                        note(v.tensor_tensor(r[1], y2_, sin, ALU.mult))
                        note(v.tensor_tensor(r[2], y2_, cos, ALU.mult))
                        link(v.tensor_tensor(r[3], y1, sin, ALU.mult))
                        note(v.tensor_tensor(y1, r[0], r[1], ALU.subtract))
                        v.tensor_tensor(y2_, r[2], r[3], ALU.add).then_inc(rope_done, 1)
                        c.tick("rope")
                        zs.append((bank_full[4 + t], c.take(4 + t)))
                    split_to(c.unit + 3)
                for half in range(2):
                    slot_uses(c)
                    split_to(c.unit + 3)
                link(v.tensor_scalar(subg[:, :], subg[:, :], lamc[:, l, 1:2], None, ALU.mult))
                for half in range(2):
                    uses = slot_uses(c)
                    split_to(c.unit + 2)
                    for t in range(TOK):
                        dve.wait_ge(bank_free[t], uses[t])
                        gs = G[:, t, half * 512:half * 512 + 512].rearrange("p (a b) -> p a b", b=VD1)
                        note(v.tensor_tensor(gs, gs, subg[:, :].unsqueeze(1).to_broadcast([P, 2, VD1]), ALU.mult))
                    split_to(c.unit + 3)
                for j in range(2):
                    ins = v.tensor_tensor_reduce(out=lvec[:, 2 * j, :], in0=lvec[:, 2 * j, :], in1=lvec[:, 2 * j + 1, :],
                                                 scale=1.0, scalar=0.0, op0=ALU.mult, op1=ALU.add,
                                                 accum_out=lams[:, j:j + 1])
                    if j == 0:
                        note(ins)
                ins.then_inc(lam_dot, 1)
                dve.wait_ge(lam_exp, l + 1)
                link(v.tensor_tensor(lams[:, 0:1], lams[:, 3:4], lams[:, 2:3], ALU.subtract))
                link(v.tensor_tensor(lams[:, 0:1], lams[:, 0:1], lamc[:, l, 0:1], ALU.subtract))

                uses = []
                for j in range(len(ATT1)):
                    uses.append([(b, c.take(b)) for b in (2 * (j % 2), 2 * (j % 2) + 1, 4 + j % 2, 6 + j % 2)])

                def maxima(j):
                    w = (ATT1[j][1] + 1) * P
                    for comp in range(2):
                        b, n = uses[j][comp]
                        dve.wait_ge(bank_full[b], n)
                        ins = v.reduce_max(ast1[:, comp, j:j + 1], bank[b][:, 0:w], AX.X)
                        note(ins)
                    settle()
                    v.tensor_scalar(ast1[:, 2:4, j:j + 1], ast1[:, 0:2, j:j + 1], -SCALE1, None, ALU.mult)\
                        .then_inc(negmax, 1)

                def mix(j):
                    w = (ATT1[j][1] + 1) * P
                    for comp in range(2):
                        b, n = uses[j][comp]
                        dve.wait_ge(bank_free[b], n)
                    link(v.reciprocal(ast1[:, 9, j:j + 1], ast1[:, 5, j:j + 1]))
                    link(v.scalar_tensor_tensor(out=ast1[:, 9, j:j + 1], in0=ast1[:, 9, j:j + 1], scalar=lams[:, 0:1],
                                                in1=ast1[:, 4, j:j + 1], op0=ALU.mult, op1=ALU.mult))
                    note(v.reciprocal(ast1[:, 6, j:j + 1], ast1[:, 4, j:j + 1]))
                    v.scalar_tensor_tensor(out=p1[:, j % 2, 0, 0:w], in0=p1[:, j % 2, 1, 0:w],
                                           scalar=ast1[:, 9, j:j + 1], in1=p1[:, j % 2, 0, 0:w],
                                           op0=ALU.mult, op1=ALU.add).then_inc(mixed, 1)

                maxima(0)
                for j in range(len(ATT1)):
                    if j + 1 < len(ATT1):
                        maxima(j + 1)
                    mix(j)
                for b in (6, 7):
                    dve.wait_ge(bank_free[b], c.uses[b])
                v.tensor_scalar(ast1[:, 7, :], ast1[:, 7, :], 1.0 / VD1, EPS, ALU.mult, ALU.add).then_inc(ms_done, 1)
                dve.wait_ge(root_done, c.tick("root"))
                link(v.reciprocal(ast1[:, 9, :], ast1[:, 8, :]))
                for i in range(TOK):
                    for h in range(HEADS1):
                        j = h * TOK + i
                        note(v.scalar_tensor_tensor(out=oall[:, j, :], in0=oall[:, j, :], scalar=ast1[:, 9, j:j + 1],
                                                    in1=G[:, i, h * VD1:h * VD1 + VD1], op0=ALU.mult, op1=ALU.mult))
                    settle()
                    om = oall[:, i:i + 13:TOK, :]
                    mm = M[:, i, :].rearrange("p (h n) -> p h n", n=VD1)
                    v.tensor_tensor(mm, mm, om, ALU.add).then_inc(m_done, 1)
                dve.wait_ge(m_done, TOK * (l + 1))
                dve.drain().then_inc(mixer_done, 1)

                left_lo(nThi, nTlo)
                add_to_x(0)
                add_to_x(1)
                dve.wait_ge(*c.x)
                norm(2 * l + 1)
                groups(GROUPS1, 1)
                dve.wait_ge(*c.x)

            norm(2 * LAYERS)

            def rotate(t, bt, n, doubled):
                heads = n // DH2
                a = rot[:, t % 2, 0, 0:n].rearrange("p (h d) -> p h d", d=DH2)
                b = rot[:, t % 2, 1, 0:n].rearrange("p (h d) -> p h d", d=DH2)
                src = bank[t][:, 0:n].rearrange("p (h d) -> p h d", d=DH2)
                half = DH2 // 2

                def row(c0, w):
                    return rope2[:, t, c0:c0 + w].unsqueeze(1).to_broadcast([P, heads, w])

                note(v.tensor_tensor(a, src, row(0, DH2), ALU.mult))
                note(v.tensor_tensor(b[:, :, 0:half], src[:, :, half:DH2], row(DH2, half), ALU.mult))
                v.tensor_tensor(b[:, :, half:DH2], src[:, :, 0:half], row(DH2 + half, half), ALU.mult)\
                    .then_inc(bank_free[t], 1)
                dve.wait_ge(bank_free[t], bt)
                if not doubled:
                    v.tensor_tensor(a, a, b, ALU.add).then_inc(rope_done, 1)
                else:
                    link(v.tensor_tensor(a, a, b, ALU.add))
                    two = rot[:, t % 2, 1, 0:doubled * P].rearrange("p (h c d) -> p h c d", c=2, d=DH2)
                    v.tensor_copy(two, a[:, 0:doubled, :].unsqueeze(2).to_broadcast([P, doubled, 2, DH2]))\
                        .then_inc(rope_done, 1)

            def rotated_slot(n=512, halves=2, side=False, doubled=0):
                uses = slot_uses(c, halves=halves)
                split_to(c.unit + 2)
                for t in range(TOK):
                    dve.wait_ge(bank_full[t], uses[t])
                    if side:
                        dve.wait_ge(side_done, c.tick("side"))
                    if len(c.turns) >= 2:
                        dve.wait_ge(*c.turns[-2])
                    rotate(t, uses[t], n, doubled)
                    c.turns.append((bank_full[4 + t], c.take(4 + t)))
                split_to(c.unit + 3)

            def attention(items, span, vw, outs, mask, scale, result):
                uses = []
                for j in range(len(items)):
                    uses.append([(b, c.take(b)) for b in (j % 4, 4 + j % 2, 6 + j % 2)])

                def maxima(j):
                    h, i = items[j]
                    w = span(i)[1]
                    o = outs(j)
                    b, n = uses[j][0]
                    dve.wait_ge(bank_full[b], n)
                    if mask is None:
                        link(v.reduce_max(ast2[:, 0, o:o + 1], bank[b][:, 0:w], AX.X))
                    else:
                        if j >= 2:
                            dve.wait_ge(bank_full[uses[j - 2][1][0]], uses[j - 2][1][1])
                        v.tensor_tensor_reduce(out=p2[:, j % 2, 0:w], in0=bank[b][:, 0:w], in1=mask(i, w), scale=1.0,
                                               scalar=PICKED, op0=ALU.add, op1=ALU.max,
                                               accum_out=ast2[:, 0, o:o + 1]).then_inc(bank_free[b], 1)
                        dve.wait_ge(bank_free[b], n)
                    v.tensor_scalar(ast2[:, 1, o:o + 1], ast2[:, 0, o:o + 1], -scale, None, ALU.mult)\
                        .then_inc(negmax, 1)

                def take_result(j):
                    b, n = uses[j][2]
                    dve.wait_ge(bank_full[b], n)
                    result(j, bank[b][:, 0:vw]).then_inc(bank_free[b], 1)

                maxima(0)
                for j in range(len(items)):
                    if j + 1 < len(items):
                        maxima(j + 1)
                    if j:
                        take_result(j - 1)
                    if mask is None:
                        dve.wait_ge(exp_done, c.n.get("exp", 0) + j + 1)
                        dve.drain().then_inc(bank_free[uses[j][0][0]], 1)
                take_result(j)
                c.tick("exp", len(items))

            def divided(items, vw):
                def result(j, o):
                    h, i = items[j]
                    link(v.reciprocal(ast2[:, 3, j:j + 1], ast2[:, 2, j:j + 1]))
                    return v.tensor_scalar(y2[:, i, h * vw:h * vw + vw], o, ast2[:, 3, j:j + 1], None, ALU.mult)
                return result

            def milestone():
                dve.drain().then_inc(stage, 1)

            def merge(b):
                left_lo(yThi, yTlo, chunks=4)
                for half in range(2):
                    uses = slot_uses(c)
                    split_to(c.unit + 2)
                    dve.wait_ge(s_bg, 16 * c.tick("bg"))
                    for t in range(TOK):
                        dve.wait_ge(bank_full[t], uses[t])
                        v.tensor_tensor(gbuf[:, t, :], bank[t][:, :], bg[:, :], ALU.add).then_inc(bank_free[t], 1)
                    dve.wait_ge(bank_free[3], uses[3])
                    dve.drain().then_inc(bias_used, 1)
                    split_to(c.unit + 3)
                    uses = slot_uses(c, halves=1)
                    split_to(c.unit + 2)
                    for t in range(TOK):
                        dve.wait_ge(sig_done, c.tick("sig"))
                        dve.wait_ge(bank_full[t], uses[t])
                        ms = merged[:, t, half * 512:half * 512 + 512]
                        if c.n["bg"] <= 2:
                            v.tensor_tensor(ms, bank[t][:, :], gbuf[:, t, :], ALU.mult).then_inc(bank_free[t], 1)
                            dve.wait_ge(bank_free[t], uses[t])
                        else:
                            v.tensor_tensor(gbuf[:, t, :], bank[t][:, :], gbuf[:, t, :], ALU.mult)\
                                .then_inc(bank_free[t], 1)
                            dve.wait_ge(bank_free[t], uses[t])
                            link(v.tensor_tensor(ms, ms, gbuf[:, t, :], ALU.add))

            c.turns = []
            dve.wait_ge(s_rope2, 16)
            for g in range(3):
                rotated_slot()
                rotated_slot()
                slot_uses(c)
                split_to(c.unit + 3)
                dve.wait_ge(s_mask, 16 * (g + 1))

                def keep(j, o):
                    h, i = DIL[j]
                    return v.tensor_copy(Og[:, g, i * 512 + h * DH2:i * 512 + h * DH2 + DH2], o)

                attention(DIL, lambda i: dil_span(g, i), DH2, lambda j: g * 32 + DIL[j][1] * 8 + DIL[j][0],
                          (lambda i, w: mask2[:, SEQ - w:SEQ]), SCALE2, keep)
                if g < 2:
                    milestone()
            mg = [ast2[:, 0, 32 * g:32 * g + 32] for g in range(3)]
            dve.wait_ge(bank_free[6], c.uses[6])
            dve.wait_ge(bank_free[7], c.uses[7])
            link(v.tensor_tensor(ast2[:, 5, 0:32], mg[0], mg[1], ALU.max))
            link(v.tensor_tensor(ast2[:, 5, 0:32], ast2[:, 5, 0:32], mg[2], ALU.max))
            for g in range(3):
                ins = v.tensor_tensor(ast2[:, 3, 32 * g:32 * g + 32], mg[g], ast2[:, 5, 0:32], ALU.subtract)
                if g < 2:
                    note(ins)
            ins.then_inc(shifted, 1)
            dve.wait_ge(raised, 1)
            link(v.tensor_tensor(ast2[:, 6, :], ast2[:, 4, :], ast2[:, 2, :], ALU.mult))
            link(v.tensor_tensor(ast2[:, 5, 0:32], ast2[:, 6, 0:32], ast2[:, 6, 32:64], ALU.add))
            link(v.tensor_tensor(ast2[:, 5, 0:32], ast2[:, 5, 0:32], ast2[:, 6, 64:96], ALU.add))
            link(v.reciprocal(ast2[:, 5, 32:64], ast2[:, 5, 0:32]))
            for g in range(3):
                note(v.tensor_tensor(ast2[:, 7, 32 * g:32 * g + 32], ast2[:, 4, 32 * g:32 * g + 32],
                                     ast2[:, 5, 32:64], ALU.mult))
            settle()
            for g in range(3):
                og_ = Og[:, g, :].rearrange("p (a d) -> p a d", d=DH2)
                note(v.tensor_tensor(og_, og_, ast2[:, 7, 32 * g:32 * g + 32].unsqueeze(2).to_broadcast([P, 32, DH2]),
                                     ALU.mult))
            settle()
            link(v.tensor_tensor(Og[:, 0, :], Og[:, 0, :], Og[:, 1, :], ALU.add))
            for t in range(TOK):
                v.tensor_tensor(y2[:, t, :], Og[:, 0, 512 * t:512 * t + 512], Og[:, 2, 512 * t:512 * t + 512], ALU.add)\
                    .then_inc(y_done, 1)
            merge(1)
            milestone()

            rotated_slot(side=True, doubled=2)
            rotated_slot(n=DH2, halves=1, side=True, doubled=1)
            rotated_slot()
            dve.wait_ge(s_mask, 16 * 4)
            link(v.tensor_copy(selb[:, 0, 0:P], mask2[:, SEQ - P:SEQ]))
            n = 0
            for i in range(1, TOK):
                w = (i + 1) * P
                sc = score[:, i % 2, 0:w]
                for h in range(4):
                    dve.wait_ge(bank_free[h], c.take(h))
                    if h == 0:
                        ins = v.tensor_scalar(sc, relu[:, h % 2, 0:w], iw[:, i, h:h + 1], None, ALU.mult)
                    else:
                        ins = v.scalar_tensor_tensor(out=sc, in0=relu[:, h % 2, 0:w], scalar=iw[:, i, h:h + 1], in1=sc,
                                                     op0=ALU.mult, op1=ALU.add)
                    ins.then_inc(relu_used, 1)
                    n += 1
                    dve.wait_ge(relu_used, n)
                link(v.tensor_tensor(sc, sc, mask2[:, SEQ - w:SEQ], ALU.add))
                for r in range(TOPK // 8):
                    link(v.max(sel8[:, :], sc))
                    link(v.match_replace(sc, sel8[:, :], sc, PICKED))
                link(v.tensor_scalar(sc, sc, PICKED / 3, NEG, ALU.is_gt, ALU.mult))
                link(v.tensor_tensor(selb[:, i, 0:w], sc, mask2[:, SEQ - w:SEQ], ALU.add))
            attention(SELA, lambda i: (0, (i + 1) * P), DH2, lambda j: j, lambda i, w: selb[:, i, 0:w], SCALE2,
                      divided(SELA, DH2))
            dve.wait_ge(bank_free[7], c.uses[7])
            for t in range(TOK):
                dve.drain().then_inc(y_done, 1)
            milestone()
            merge(0)
            milestone()

            dve.wait_ge(s_mem, 16)
            mean_roots(2, D)
            for t in range(2):
                v.tensor_scalar(memx[:, t, :], memx[:, t, :], stat[:, 2, t:t + 1], None, ALU.mult).then_inc(xn_done, 1)
            left_lo(memhi, memlo, 2 * LAYERS + 2, n=MEM)
            for tiles in (4, 2, 4):
                slot_uses(c, tiles)
                split_to(c.unit + 3)
            attention(MEMA, lambda i: (0, MEM), P, lambda j: j, None, SCALE_M, divided(MEMA, P))
            dve.wait_ge(bank_free[7], c.uses[7])
            for t in range(TOK):
                dve.drain().then_inc(y_done, 1)
            merge(2)
            milestone()
            left_lo(nThi, nTlo)
            add_to_x(0)
            add_to_x(1)
            dve.wait_ge(*c.x)
            milestone()

            norm(2 * LAYERS + 1)
            dve.wait_ge(wr_hi, 1)
            v.tensor_tensor(wrlo[:, :, :], wr[:, :, :], wrhi[:, :, :].bitcast(F32), ALU.subtract).then_inc(wr_lo, 1)
            for t in range(TOK):
                dve.wait_ge(bank_full[t], c.take(t))
                v.tensor_tensor(sl[:, t, :], bank[t][:, 0:20], rb[:, :], ALU.add).then_inc(bank_free[t], 1)
            dve.wait_ge(bank_free[3], c.uses[3])

            def each(r, w=4):
                return rt[:, r, :, 0:w]

            def over(a, w=4):
                return a.to_broadcast([P, TOK, w])

            def first_best(src, best, hot, seen):
                link(v.tensor_reduce(each(best, 1), src, AX.X, ALU.max))
                link(v.tensor_tensor(each(hot), src, over(each(best, 1)), ALU.is_ge))
                link(v.tensor_scalar(each(seen, 1), rt[:, hot, :, 0:1], -1.0, 1.0, ALU.mult, ALU.add))
                for j in range(1, 4):
                    link(v.tensor_tensor(rt[:, hot, :, j:j + 1], rt[:, hot, :, j:j + 1], each(seen, 1), ALU.mult))
                    link(v.tensor_tensor(each(seen, 1), each(seen, 1), rt[:, hot, :, j:j + 1], ALU.subtract))

            first_best(sl[:, :, 0:4], 2, 3, 4)
            v.tensor_tensor(each(0), sl[:, :, 0:4], over(each(2, 1)), ALU.subtract).then_inc(shifted, 1)
            dve.wait_ge(raised, 2)
            link(v.tensor_reduce(each(5, 1), each(1), AX.X, ALU.add))
            link(v.reciprocal(each(5, 1), each(5, 1)))
            for g in range(4):
                link(v.tensor_tensor(each(6 if g == 0 else 7), sl[:, :, 4 + 4 * g:8 + 4 * g],
                                     over(rt[:, 3, :, g:g + 1]), ALU.mult))
                if g:
                    link(v.tensor_tensor(each(6), each(6), each(7), ALU.add))
            first_best(each(6), 10, 11, 4)
            link(v.scalar_tensor_tensor(out=each(7), in0=each(11), scalar=PICKED, in1=each(6), op0=ALU.mult,
                                        op1=ALU.add))
            first_best(each(7), 12, 13, 4)
            v.tensor_tensor(each(8, 1), each(12, 1), each(10, 1), ALU.subtract).then_inc(shifted, 1)
            dve.wait_ge(raised, 3)
            link(v.tensor_scalar(each(14, 1), each(9, 1), 1.0, None, ALU.add))
            link(v.reciprocal(each(14, 1), each(14, 1)))
            link(v.tensor_tensor(each(14, 1), each(14, 1), each(5, 1), ALU.mult))
            link(v.tensor_tensor(each(15, 1), each(14, 1), each(9, 1), ALU.mult))
            link(v.tensor_tensor(each(11), each(11), over(each(14, 1)), ALU.mult))
            link(v.tensor_tensor(each(13), each(13), over(each(15, 1)), ALU.mult))
            link(v.tensor_tensor(each(11), each(11), each(13), ALU.add))
            for g in range(4):
                link(v.tensor_tensor(comb[:, :, 4 * g:4 * g + 4], each(11), over(rt[:, 3, :, g:g + 1]), ALU.mult))
            groups(GROUPS2, 2, weight=lambda t, e: comb[:, t, bass.ds(e, 1)])
            dve.wait_ge(*c.x)

            mean_roots(TOK, D)
            dve.wait_ge(s_g, 16)
            for t in range(TOK):
                v.scalar_tensor_tensor(out=xn[:, t, :], in0=x[:, t, :], scalar=stat[:, 2, t:t + 1], in1=og[:, :],
                                       op0=ALU.mult, op1=ALU.mult).then_inc(out_done, 1)


_INS = ["x", "w_in", "q_norm_g", "k_norm_g", "lam_q1", "lam_k1", "lam_q2", "lam_k2", "subln_g", "pool_w", "pool_scale",
        "w_out", "w_ffn_in", "w_ffn_out", "mem_2", "w_in_2", "w_mem_kv_2", "w_gate_2", "b_gate_2", "w_branch_2",
        "w_out_2", "w_group_2", "b_group_2", "w_sub_2", "b_sub_2", "w1_2", "w3_2", "w2_2", "g_final_2"]


def kernel(**inputs):
    import concourse.bacc as bacc
    from concourse.bass_utils import run_bass_kernel_spmd

    arrays = {name: np.ascontiguousarray(inputs[name]) for name in _INS}
    gains = [np.asarray(inputs[n])[l] for l in range(LAYERS) for n in ("norm1_g", "norm2_g")]
    gains += [np.asarray(inputs[n])[0] for n in ("g_mix_2", "g_ffn_2", "g_mem_2")]
    arrays["c_gains"] = np.ascontiguousarray(np.stack([g.reshape(KT, P).T for g in gains], axis=1))
    arrays.update(host_constants())
    nc = bacc.Bacc("TRN2", target_bir_lowering=False, num_devices=1)
    A = {n: nc.dram_tensor("in_" + n, a.shape, mybir.dt.from_np(a.dtype), kind="ExternalInput").ap()
         for n, a in arrays.items()}
    out = nc.dram_tensor("out", (1, SEQ, D), F32, kind="ExternalOutput").ap()
    build(nc, A, out)
    r = run_bass_kernel_spmd(nc, [{"in_" + n: a for n, a in arrays.items()}], core_ids=[0])
    return r.results[0]["out"]
```

```python
from contextlib import ExitStack
from math import exp as math_exp

import numpy as np
import concourse.bass as bass
from concourse import mybir

F32 = mybir.dt.float32
F32R = mybir.dt.float32r
ALU = mybir.AluOpType
ACT = mybir.ActivationFunctionType
AX = mybir.AxisListType

P = 128
SEQ = 512
TOK = SEQ // P
D = 1024
KT = D // P
LAYERS = 2
CHUNK = 64
EPS = 1e-6
NEG = -1e30

DH1 = 128
HEADS1 = 4
VD1 = 256
ROT_HALF = 16
SCALE1 = DH1 ** -0.5
POOL_WINDOWS = (2, 4, 8, 16)
HID1 = 2816
GROUPS1 = HID1 // 256

DH2 = 64
SCALE2 = DH2 ** -0.5
SCALE_M = 128 ** -0.5
MEM = 256
TOPK = 128
PICKED = -3e38
EXPERTS = 16
HID2 = 512
ROUTES = 20
CHUNKS = (2 * SEQ + EXPERTS * (P - 1)) // P + 1
AQ, AK, AV, IQ, IK, IW, BQ, BK, BV, MQ = 0, 512, 640, 768, 1024, 1088, 1092, 2628, 4164, 5700

RING = 3
UNIT = 2048
LAYER_UNITS = 2 * 12 + 1 + 2 * 2 + 3 * GROUPS1
NARROW_UNIT = LAYERS * LAYER_UNITS + 3 * 6 + 6 + 2
STATIC_UNITS = NARROW_UNIT + 1 + 2 + 6 + 6 + 6 + 4


def host_constants():
    pos = np.arange(SEQ, dtype=np.float32)

    def table(theta, half, width):
        e = (np.arange(half, dtype=np.float32) * np.float32(1.0)) / np.float32(half)
        inv = (np.float32(theta) ** (-e)).astype(np.float32)
        ang = (pos[:, None] * inv[None, :]).astype(np.float32)
        return np.cos(ang).astype(np.float32), np.sin(ang).astype(np.float32)

    def tiles(a):
        return np.ascontiguousarray(a.reshape(TOK, P, -1).transpose(1, 0, 2))

    c1, s1 = table(500000.0, ROT_HALF, 16)
    c2, s2 = table(10000.0, DH2 // 2, 32)
    rope1 = np.concatenate([tiles(c1), tiles(s1)], axis=2)
    rope2 = np.concatenate([tiles(np.concatenate([c2, c2], 1)), tiles(np.concatenate([-s2, s2], 1))], axis=2)
    q, k = np.arange(P)[:, None], np.arange(P)[None, :]
    neg = lambda keep: np.where(keep, 0.0, NEG).astype(np.float32)
    causal = neg(k <= q)
    free = np.zeros((P, P), np.float32)
    masks = np.stack([
        np.concatenate([free, free, neg(k >= q), causal], 1),
        np.concatenate([free, free, free, causal], 1),
        np.concatenate([free, free, free, neg(((q - k) % 4 == 0) & (k <= q))], 1),
        np.concatenate([free, free, free, causal], 1),
    ]).astype(np.float32)
    chunk = neg(q // CHUNK >= k // CHUNK)
    count = np.stack([1.0 / np.minimum(pos + 1.0, float(w)) for w in POOL_WINDOWS]).astype(np.float32)
    lam = np.array([[0.8 - 0.6 * math_exp(-0.3 * i), 1.0 - (0.8 - 0.6 * math_exp(-0.3 * i))]
                    for i in range(LAYERS)], np.float32)
    before = (q < k).astype(np.float32)
    steps = np.stack([np.arange(CHUNKS) * P, np.arange(CHUNKS)]).astype(np.float32)
    return {"c_before": before, "c_slots": np.arange(P, dtype=np.float32), "c_steps": steps,
            "c_ident": np.eye(P, dtype=np.float32), "c_rope1": rope1, "c_rope2": rope2, "c_masks": masks,
            "c_chunk": chunk, "c_count": count, "c_lam": lam}


def build(nc, A, out):
    with ExitStack() as ctx:
        def sb(name, shape, dt=F32):
            return ctx.enter_context(nc.sbuf_tensor(name, shape, dt))

        def sem(name):
            return ctx.enter_context(nc.semaphore(name))

        def at(kb, name, shape, dt=F32):
            with ExitStack() as turn:
                if kb:
                    turn.enter_context(nc.sbuf_tensor("before_" + name, [P, int(kb * 256)], F32))
                return turn.enter_context(nc.sbuf_tensor(name, shape, dt))

        ident = sb("ident", [P, P])
        x = sb("x", [P, TOK, D])
        oall = at(0, "oall", [P, 16, VD1])
        p1 = at(16, "p1", [P, 2, 2, SEQ])
        pt1 = at(24, "pt1", [P, 2, SEQ])
        nThi = sb("nThi", [P, KT, SEQ], F32R)
        nTlo = sb("nTlo", [P, KT, SEQ], F32R)
        raw = sb("raw", [P, RING, UNIT])
        whi = sb("whi", [P, RING, UNIT], F32R)
        wlo = sb("wlo", [P, RING, UNIT], F32R)
        gcol = sb("gcol", [P, 2 * LAYERS + 3, KT])
        stat = sb("stat", [P, 3, 4])
        countw = sb("countw", [P, 4, 16])
        lamc = sb("lamc", [P, LAYERS, 2])
        lams = sb("lams", [P, 4])
        sel8 = sb("sel8", [P, 8])
        iw = sb("iw", [P, TOK, 4])

        M = at(0, "M", [P, TOK, D])
        G = at(16, "G", [P, TOK, D])
        qT = at(32, "qT", [P, 8, SEQ])
        kT = at(48, "kT", [P, 8, SEQ])
        v1 = at(64, "v1", [P, TOK, D])
        qsq = at(16, "qsq", [P, SEQ])
        qy = at(18, "qy", [P, 2, SEQ])
        qrot = at(22, "qrot", [P, 4, 4 * ROT_HALF])
        qst = at(23, "qst", [P, 3, 4])
        win = at(32, "win", [P, 4, SEQ + 16])
        prow = at(41, "prow", [P, D])
        poolhi = at(48, "poolhi", [P, KT, SEQ], F32R)
        poollo = at(64, "poollo", [P, KT, SEQ], F32R)
        qkg = at(80, "qkg", [P, 2, DH1])
        chunkm = at(81, "chunkm", [P, P])
        rope1 = at(81.5, "rope1", [P, TOK, 2 * ROT_HALF])
        subg = at(82, "subg", [P, VD1])
        lvec = at(83, "lvec", [P, 4, DH1])
        qst16 = at(23.5, "qst16", [P, 16])
        ast1 = at(85, "ast1", [P, 10, 16])
        xn = at(0, "xn", [P, TOK, D])
        hf = at(0, "hf", [P, 2, SEQ])
        sg = at(4, "sg", [P, 2, SEQ])
        hhi = at(8, "hhi", [P, 2, SEQ], F32R)
        hlo = at(12, "hlo", [P, 2, SEQ], F32R)
        y2 = at(0, "y2", [P, TOK, 512])
        rot = at(8, "rot", [P, 2, 2, SEQ])
        yThi = at(8, "yThi", [P, 4, SEQ], F32R)
        yTlo = at(16, "yTlo", [P, 4, SEQ], F32R)
        mask2 = at(16, "mask2", [P, SEQ])
        ast2 = at(18, "ast2", [P, 8, 96])
        merged = at(24, "merged", [P, TOK, D])
        gbuf = at(40, "gbuf", [P, TOK, 512])
        p2 = at(76, "p2", [P, 2, SEQ])
        pt2 = at(80, "pt2", [P, 2, SEQ])
        rope2 = at(84, "rope2", [P, TOK, 2 * DH2])
        bq = at(24, "bq", [P, 4, SEQ])
        bk = at(32, "bk", [P, 4, SEQ])
        bv = at(40, "bv", [P, TOK, 512])
        Og = at(48, "Og", [P, 3, TOK * 512])
        score = [at(kb, f"score{i}", [P, SEQ]) for i, kb in enumerate((40, 42, 8), 1)]
        relu = at(44, "relu", [P, 2, SEQ])
        aq = at(48, "aq", [P, 4, SEQ])
        ak = at(56, "ak", [P, 2, SEQ])
        av = at(60, "av", [P, TOK, P])
        iqT = at(62, "iqT", [P, 2, SEQ])
        ik = at(66, "ik", [P, SEQ])
        selb = at(68, "selb", [P, TOK, SEQ])
        memx = at(8, "memx", [P, 2, D])
        memhi = at(48, "memhi", [P, KT, MEM], F32R)
        memlo = at(56, "memlo", [P, KT, MEM], F32R)
        km = at(64, "km", [P, 4, MEM])
        vm = at(68, "vm", [P, 2, 512])
        mqT = at(40, "mqT", [P, 4, SEQ])
        bg = at(72, "bg", [P, 512])
        wr = at(20, "wr", [P, KT, ROUTES])
        wrhi = at(21, "wrhi", [P, KT, ROUTES], F32R)
        wrlo = at(22, "wrlo", [P, KT, ROUTES], F32R)
        rt = at(24, "rt", [P, 16, TOK, 4])
        routeT = at(76, "routeT", [ROUTES, SEQ])
        sl = at(28, "sl", [P, TOK, ROUTES])
        rb = at(23, "rb", [P, ROUTES])
        og = at(16, "og", [P, D])
        stat0 = at(21.5, "stat0", [P, 2, TOK * 8])
        memj = at(16, "memj", [P, 2, D])
        I32 = mybir.dt.int32
        ch = at(30, "ch", [P, 8, EXPERTS])
        keys = at(31, "keys", [P, TOK, CHUNKS])
        wts = at(32, "wts", [P, TOK, CHUNKS])
        rel = at(33, "rel", [P, 5, TOK * CHUNKS])
        ep = at(35, "ep", [P, 5, TOK, EXPERTS])
        ecmp = at(37, "ecmp", [P, CHUNKS, EXPERTS])
        efl = at(39, "efl", [P, CHUNKS + 1])
        ids = at(39.25, "ids", [P, CHUNKS + 1], I32)
        spot = at(39.5, "spot", [P, 2, TOK])
        xghi = at(40, "xghi", [P, KT, P], F32R)
        xglo = at(44, "xglo", [P, KT, P], F32R)
        mh = at(48, "mh", [P, HID2])
        msg = at(50, "msg", [P, HID2])
        hthi = at(52, "hthi", [P, 4, P], F32R)
        htlo = at(54, "htlo", [P, 4, P], F32R)
        yhi = at(56, "yhi", [P, D], F32R)
        ylo = at(60, "ylo", [P, D], F32R)
        hot = at(64, "hot", [P, TOK, P])
        hotT = at(66, "hotT", [P, SEQ], F32R)
        tri = at(68, "tri", [P, P])
        ones = at(68.5, "ones", [P, P])
        slots = at(69, "slots", [P, P])
        steps = at(69.5, "steps", [P, 2, CHUNKS])
        more = at(70, "more", [P, 2, UNIT], F32R)

        def parts(U, j):
            j %= 6
            if j < 3:
                return whi[:, (U + j) % RING, :], wlo[:, (U + j) % RING, :]
            if j == 5:
                return more[:, 0, :], more[:, 1, :]
            both = (nThi, nTlo)[j - 3]
            return tuple(both[:, k:k + 4, :].rearrange("p k n -> p (k n)") for k in (0, 4))
        sb("arena", [P, 86 * 256])

        bank = [ctx.enter_context(nc.psum_tensor(f"bank{b}", [P, 512], F32)) for b in range(8)]

        raw_full = [sem(f"raw_full{i}") for i in range(RING)]
        hi_done = sem("hi_done")
        split_done = sem("split_done")
        first_half = sem("first_half")
        bank_full = [sem(f"bank_full{b}") for b in range(8)]
        bank_free = [sem(f"bank_free{b}") for b in range(8)]
        s_x = sem("x_landed")
        s_first = sem("identity_and_gains_landed")
        s_const = sem("const_landed")
        s_layer = sem("layer_rows_landed")
        s_rope2 = sem("rope2_landed")
        s_mask = sem("mask_landed")
        s_bg = sem("bg_landed")
        s_mem = sem("mem_landed")
        s_residue = sem("residue_order_landed")
        s_route = sem("route_landed")
        s_g = sem("final_gain_landed")
        s_store = sem("stored")
        chain = sem("vector_chain")
        sq_done = sem("sq_done")
        ms_done = sem("ms_done")
        root_done = sem("root_done")
        xn_done = sem("xn_done")
        nhi_done = sem("nhi_done")
        mixer_done = sem("mixer_done")
        pooled = sem("pooled")
        poolhi_done = sem("poolhi_done")
        poollo_done = sem("poollo_done")
        qsq_done = sem("qsq_done")
        qms_done = sem("qms_done")
        qroot_done = sem("qroot_done")
        rope_done = sem("rope_done")
        lam_dot = sem("lam_dot")
        lam_exp = sem("lam_exp")
        negmax = sem("negmax")
        mixed = sem("mixed")
        m_done = sem("m_done")
        pad_zero = sem("pad_zero")
        hhi_done = sem("hhi_done")
        hlo_done = sem("hlo_done")
        side_done = sem("side_done")
        relu_used = sem("relu_used")
        exp_done = sem("exp_done")
        y_done = sem("y_done")
        stage = sem("stage")
        bias_used = sem("bias_used")
        sig_done = sem("sig_done")
        shifted = sem("shifted")
        raised = sem("raised")
        wr_hi = sem("wr_hi")
        wr_lo = sem("wr_lo")
        out_done = sem("out_done")
        ones_done = sem("ones_done")
        s_tables = sem("expert_constants_landed")
        member = sem("member")
        placed = sem("placed")
        hot_done = sem("hot_done")
        ht_hi = sem("ht_hi_done")
        y_hi = sem("y_hi_done")
        x_final = sem("x_final")

        class Ledger:

            def __init__(self):
                self.unit = 0
                self.split = 0
                self.halves = 0
                self.uses = [0] * 8
                self.released = []
                self.n = {}
                self.x = [(s_x, 16)] * TOK

            def take(self, b):
                self.uses[b] += 1
                return self.uses[b]

            def half(self):
                self.halves += 1
                self.unit += 1
                self.released.append((first_half, self.halves))

            def full(self, b, n):
                self.unit += 1
                self.released.append((bank_full[b], n))

            def tick(self, name, k=1):
                self.n[name] = self.n.get(name, 0) + k
                return self.n[name]

        def cols(w, c0, width=512):
            v = w[:, c0:c0 + width].rearrange("(k p) n -> p k n", p=P)
            for half in range(2):
                yield [(k * width, v[:, 4 * half + k:4 * half + k + 2, :], 2, width) for k in (0, 2)]

        def units_before_groups(l):
            w = A["w_in"][l]
            for c in (0, 1, 8, 9):
                yield from cols(w, c * 512)
            pw = A["pool_w"][l].rearrange("g (k p) n -> p (g k) n", p=P)
            yield [(k * 256, pw[:, k:k + 4, :], 4, 256) for k in (0, 4)]
            for c in (2, 3, 4, 5, 6, 7, 10, 11):
                yield from cols(w, c * 512)
            for c in range(2):
                yield from cols(A["w_out"][l], c * 512)

        def units_second():
            w = A["w_in_2"][0]
            wg = A["w_gate_2"][0]

            def branch(b):
                for half in range(2):
                    yield from cols(wg, b * D + half * 512)
                    v = A["w_branch_2"][0, b].rearrange("(k p) n -> p k n", p=P)[:, :, half * 512:half * 512 + 512]
                    yield [(k * 512, v[:, k:k + 2, :], 2, 512) for k in (0, 2)]

            for g in range(3):
                for c in (BQ, BK, BV):
                    yield from cols(w, c + g * 512)
            yield from branch(1)
            yield from cols(w, AK)
            v = w[:, IK:IK + 68].rearrange("(k p) n -> p k n", p=P)
            yield [(k * 68, v[:, k:k + 4, :], 4, 68) for k in (0, 4)]
            yield from cols(w, AQ)
            yield from branch(0)
            yield from cols(w, MQ)
            yield from cols(A["w_mem_kv_2"][0], 0)
            yield from cols(A["w_mem_kv_2"][0], 512)
            yield from branch(2)
            for c in range(2):
                yield from cols(A["w_out_2"][0], c * 512)

        block = ctx.enter_context(nc.Block())

        @block.sync
        def _(sp):
            c = Ledger()

            def load(s, parts):
                for off, src, k, width in parts:
                    dst = raw[:, s, off:off + k * width].rearrange("p (k n) -> p k n", k=k)
                    sp.dma_start(dst, src).then_inc(raw_full[s], 16)

            def unit(parts):
                if c.unit >= RING:
                    sp.wait_ge(split_done, c.unit - RING + 1)
                load(c.unit % RING, parts)
                c.unit += 1

            def group_in(s0, base, w_gate, w_up):
                for half in range(2):
                    s = (s0 + half) % RING
                    if base is not None:
                        sp.wait_ge(split_done, base + half)
                    for j, w in enumerate((w_gate, w_up)):
                        src = w.rearrange("(k p) n -> p k n", p=P)[:, 4 * half:4 * half + 4, :]
                        dst = raw[:, s, :].rearrange("p (k n) -> p k n", k=4)[:, :, 256 * j:256 * j + 256]
                        sp.dma_start(dst, src).then_inc(raw_full[s], 16)

            def group_out(s, base, w_down):
                sp.wait_ge(split_done, base)
                src = w_down.rearrange("(k p) n -> p k n", p=P)
                for k in (1, 0):
                    sp.dma_start(raw[:, s, k * D:k * D + D], src[:, k, :]).then_inc(raw_full[s], 16)

            sp.dma_start(x[:, :, :], A["x"][0].rearrange("(t p) d -> p t d", p=P)).then_inc(s_x, 16)
            for l in range(LAYERS):
                for parts in units_before_groups(l):
                    unit(parts)
                w1, w2 = A["w_ffn_in"][l], A["w_ffn_out"][l]
                u = c.unit
                group_in(u % RING, u - 2, w1[:, 0:256], w1[:, HID1:HID1 + 256])
                with sp.Fori(0, GROUPS1 - 1) as g:
                    group_in((u + 2) % RING, u + 3 * g,
                             w1[:, bass.ds(256 * g + 256, 256)], w1[:, bass.ds(HID1 + 256 + 256 * g, 256)])
                    group_out((u + 4) % RING, u + 3 * g + 2, w2[bass.ds(256 * g, 256), :])
                group_out((u + 2) % RING, u + 3 * GROUPS1 - 3, w2[HID1 - 256:HID1, :])
                c.unit += 3 * GROUPS1
            for parts in units_second():
                unit(parts)
            w1, w3 = (A[n][0].rearrange("e (k p) n -> e p k n", p=P) for n in ("w1_2", "w3_2"))
            w2 = A["w2_2"][0].rearrange("e (k p) n -> e p k n", p=P)
            u = c.unit

            def expert_of(i):
                return sp.value_load(ids[0:1, i:i + 1] if isinstance(i, int) else ids[0:1, bass.ds(i, 1)],
                                     min_val=0, max_val=EXPERTS - 1)

            def expert_unit(j, base, e):
                s = (u + j) % RING
                sp.wait_ge(split_done, base + j - 2)
                w, k, nk = ((w1, 0, 4), (w1, 4, 4), (w3, 0, 4), (w3, 4, 4), (w2, 0, 2), (w2, 2, 2))[j]
                width = UNIT // nk
                for k0 in (nk // 2, 0):
                    dst = raw[:, s, k0 * width:(k0 + nk // 2) * width].rearrange("p (k n) -> p k n", n=width)
                    sp.dma_start(dst, w[e, :, k + k0:k + k0 + nk // 2, :]).then_inc(raw_full[s], 16)

            sp.wait_ge(placed, 1)
            chunks = sp.value_load(ids[0:1, CHUNKS:CHUNKS + 1], min_val=SEQ * 2 // P, max_val=CHUNKS - 1)
            e = expert_of(0)
            for j in range(5):
                expert_unit(j, u, e)
            with sp.Fori(0, chunks) as i:
                e = expert_of(i)
                after = expert_of(i + 1)
                expert_unit(5, u + 6 * i, e)
                for j in range(5):
                    expert_unit(j, u + 6 * i + 6, after)
            for t in range(TOK):
                sp.wait_ge(out_done, t + 1)
                sp.dma_start(out[0, t * P:(t + 1) * P, :], xn[:, t, :]).then_inc(s_store, 16)
            sp.wait_ge(s_store, 16 * TOK)

        @block.gpsimd
        def _(pool):
            def rows(dst, src, s):
                pool.dma_start(dst, src).then_inc(s, 16)

            def gate_bias(b, half):
                c0 = b * D + half * 512
                rows(bg[:, :], A["b_gate_2"][0, c0:c0 + 512].partition_broadcast(P), s_bg)

            rows(ident[:, :], A["c_ident"], s_first)
            rows(gcol[:, :, :], A["c_gains"], s_first)
            rows(chunkm[:, :], A["c_chunk"], s_const)
            rows(rope1[:, :, :], A["c_rope1"], s_const)
            rows(countw[:, :, :], A["c_count"][:, 0:16].partition_broadcast(P), s_const)
            rows(lamc[:, :, :], A["c_lam"].partition_broadcast(P), s_const)
            for l in range(LAYERS):
                if l:
                    pool.wait_ge(mixer_done, l)
                rows(prow[:, :], A["pool_scale"][l].partition_broadcast(P), s_layer)
                rows(qkg[:, 0, :], A["q_norm_g"][l].partition_broadcast(P), s_layer)
                rows(qkg[:, 1, :], A["k_norm_g"][l].partition_broadcast(P), s_layer)
                rows(subg[:, :], A["subln_g"][l].partition_broadcast(P), s_layer)
                for j, name in enumerate(("lam_q1", "lam_k1", "lam_q2", "lam_k2")):
                    rows(lvec[:, j, :], A[name][l].partition_broadcast(P), s_layer)
            pool.wait_ge(mixer_done, LAYERS)
            rows(rope2[:, :, :], A["c_rope2"], s_rope2)
            rows(mask2[:, :], A["c_masks"][0], s_mask)
            gate_bias(1, 0)
            for g in (1, 2):
                pool.wait_ge(stage, g)
                rows(mask2[:, :], A["c_masks"][g], s_mask)
                if g == 1:
                    for t in range(TOK):
                        for res in range(TOK):
                            to, fr = slice(32 * t, 32 * t + 32), slice(res, P, TOK)
                            rows(y2[to, res, :], Og[fr, 0, 512 * t:512 * t + 512], s_residue)
                            rows(stat0[to, :, 8 * res:8 * res + 8], ast2[fr, 0:3:2, 8 * t:8 * t + 8], s_residue)
            pool.wait_ge(bias_used, 1)
            gate_bias(1, 1)
            pool.wait_ge(stage, 3)
            rows(mask2[:, :], A["c_masks"][3], s_mask)
            pool.wait_ge(stage, 4)
            gate_bias(0, 0)
            pool.wait_ge(bias_used, 3)
            gate_bias(0, 1)
            pool.wait_ge(stage, 5)
            rows(memx[:, :, :], A["mem_2"][0].rearrange("(t p) d -> p t d", p=P), s_mem)
            gate_bias(2, 0)
            pool.wait_ge(bias_used, 5)
            gate_bias(2, 1)
            pool.wait_ge(stage, 6)
            rows(wr[:, :, 0:4], A["w_group_2"][0].rearrange("(k p) n -> p k n", p=P), s_route)
            for g in range(4):
                rows(wr[:, :, 4 + 4 * g:8 + 4 * g], A["w_sub_2"][0, g].rearrange("(k p) n -> p k n", p=P), s_route)
            rows(rb[:, 0:4], A["b_group_2"][0].partition_broadcast(P), s_route)
            rows(rb[:, 4:20], A["b_sub_2"][0].rearrange("g e -> (g e)").partition_broadcast(P), s_route)
            rows(tri[:, :], A["c_before"], s_tables)
            rows(slots[:, :], A["c_slots"].partition_broadcast(P), s_tables)
            rows(steps[:, :, :], A["c_steps"].partition_broadcast(P), s_tables)
            pool.memset(ones[:, :], 1.0).then_inc(ones_done, 1)
            rows(og[:, :], A["g_final_2"].partition_broadcast(P), s_g)

        def slot_uses(c, tiles=4, halves=2):
            n = [c.take(j) for j in range(tiles)]
            if halves == 2:
                c.half()
            c.full(tiles - 1, n[-1])
            return n

        def groups_begin(c, n):
            before = Before()
            before.unit, before.halves, before.uses, before.n = c.unit, c.halves, list(c.uses), n
            before.h = c.n.get("h", 0)
            return before

        def groups_end(c, w):
            for g in range(w.n):
                c.released.append((first_half, w.halves + g + 1))
                c.released.append((bank_full[3], w.uses[3] + g + 1))
                if g:
                    c.released.append((bank_full[7], w.uses[7] + 2 * g))
            c.released.append((bank_full[7], w.uses[7] + 2 * w.n))
            c.unit += 3 * w.n
            c.halves += w.n
            c.uses = [u + (w.n if b < 4 else 2 * w.n) for b, u in enumerate(c.uses)]
            c.tick("h", w.n)
            c.x = []
            for t in range(TOK):
                b, turn = 4 + (2 * t + 1) % 4, (2 * t + 1) // 4
                c.x.append((bank_free[b], c.uses[b] - 1 + turn))

        class Before:
            pass

        def in_order(out, src):
            return out, src

        def from_residues(out, src):
            return out.rearrange("p (j r) -> p r j", r=TOK), src.rearrange("p (r j) -> p r j", r=TOK)

        ATT1 = [(h, i) for h in range(HEADS1) for i in range(TOK)]
        DIL = [(h, i) for i in range(TOK) for h in range(8)]
        SELA = [(h, i) for i in range(TOK) for h in range(8)]
        MEMA = [(h, i) for i in range(TOK) for h in range(4)]

        def dil_span(g, i):
            if g == 0:
                return max(0, i - 1) * P, min(i + 1, 2) * P
            return i * P, P

        def dil_cols(g, c0, w):
            return slice(c0, c0 + w) if g == 0 else slice(c0 // P, SEQ, TOK)

        @block.tensor
        def _(pe):
            c = Ledger()

            def take(b):
                n = c.take(b)
                if n > 1:
                    pe.wait_ge(bank_free[b], n - 1)
                return bank[b]

            def product(o, lh, ll, rh, rl, first, last):
                nc.tensor.matmul(o, lh, rh, start=first, stop=False)
                nc.tensor.matmul(o, lh, rl, start=False, stop=False)
                return nc.tensor.matmul(o, ll, rh, start=False, stop=last)

            def wait_unit():
                pe.wait_ge(split_done, c.unit + 1)
                return c.unit % RING

            left_written = []

            def wait_left(k):
                if k < len(left_written):
                    pe.wait_ge(*left_written[k])

            def slot(orient, hook=None, left=(nThi, nTlo), tiles=4, n=512, width=512, halves=2,
                     tokens=lambda j: slice(j * P, j * P + P)):
                lhi, llo = left
                for half in range(halves):
                    s = wait_unit()
                    for j in range(tiles):
                        if half == 0:
                            take(j)
                        nk = 4 if width == 512 else KT
                        for kk in range(nk):
                            k = 4 * half + kk
                            w0 = kk * width
                            if j == 0:
                                wait_left(k)
                            if orient == "tok":
                                lt = tokens(j)
                                last = product(bank[j][:, 0:width], lhi[:, k, lt], llo[:, k, lt],
                                               whi[:, s, w0:w0 + width], wlo[:, s, w0:w0 + width],
                                               half == 0 and kk == 0, half == halves - 1 and kk == nk - 1)
                            else:
                                w0 += j * P
                                last = product(bank[j][:, 0:n], whi[:, s, w0:w0 + P], wlo[:, s, w0:w0 + P],
                                               lhi[:, k, 0:n], llo[:, k, 0:n],
                                               half == 0 and kk == 0, half == halves - 1 and kk == nk - 1)
                        if half == halves - 1:
                            last.then_inc(bank_full[j], 1)
                        elif j == tiles - 1:
                            last.then_inc(first_half, 1)
                        if half == 0 and hook:
                            hook(j)
                    if half == halves - 1:
                        c.full(tiles - 1, c.uses[tiles - 1])
                        left_written.clear()
                    else:
                        c.half()

            def to_feature_major(src, tiles, ready, chunks=KT, n0=0):
                left_written.clear()
                for k in range(chunks):
                    b = 4 + k % 4
                    take(b)
                    left_written.append((bank_free[b], c.uses[b]))
                    for t in range(tiles):
                        if k == 0 and ready:
                            pe.wait_ge(ready, n0 + t + 1)
                        last = nc.tensor.transpose(bank[b][:, t * P:t * P + P], src[:, t, k * P:k * P + P], ident[:, :])
                    last.then_inc(bank_full[b], 1)

            def head_turns(z, t, views, ready):
                b = 4 + t
                take(b)
                pe.wait_ge(ready, z + 1)
                for j, v in enumerate(views):
                    last = nc.tensor.transpose(bank[b][:, j * P:j * P + P], v, ident[:, :])
                last.then_inc(bank_full[b], 1)

            def groups(n):
                w = groups_begin(c, n)

                def into(g):
                    for half in range(2):
                        first = w.unit if isinstance(g, int) and g == 0 else w.unit + 3 * g - 1
                        s = (w.unit + half + (0 if isinstance(g, int) and g == 0 else 2)) % RING
                        pe.wait_ge(split_done, first + half + 1)
                        for j in range(4):
                            if half == 0:
                                pe.wait_ge(bank_free[j], w.uses[j] + g)
                            for kk in range(4):
                                k, w0 = 4 * half + kk, kk * 512 + j * P
                                if isinstance(g, int) and g == 0 and j == 0:
                                    wait_left(k)
                                last = product(bank[j][:, :], whi[:, s, w0:w0 + P], wlo[:, s, w0:w0 + P],
                                               nThi[:, k, :], nTlo[:, k, :], k == 0, k == KT - 1)
                            if half:
                                last.then_inc(bank_full[j], 1)
                        if not half:
                            last.then_inc(first_half, 1)

                def outof(g, unit, s):
                    pe.wait_ge(split_done, unit + 1)
                    pe.wait_ge(hlo_done, w.h + g + 1)
                    for tile in range(8):
                        t, half, b = tile // 2, tile % 2, 4 + tile % 4
                        pe.wait_ge(bank_free[b], w.uses[b] + 2 * g + tile // 4)
                        for kk in range(2):
                            w0 = kk * D + half * 512
                            last = product(bank[b][:, :], hhi[:, kk, t * P:t * P + P], hlo[:, kk, t * P:t * P + P],
                                           whi[:, s, w0:w0 + 512], wlo[:, s, w0:w0 + 512], kk == 0, kk == 1)
                        last.then_inc(bank_full[b], 1)

                into(0)
                with pe.Fori(0, n - 1) as g:
                    into(g + 1)
                    outof(g, w.unit + 3 * g + 4, (w.unit + 4) % RING)
                outof(n - 1, w.unit + 3 * n - 1, (w.unit + 3 * n - 1) % RING)
                groups_end(c, w)

            pe.wait_ge(s_first, 16 * 2)
            for l in range(LAYERS):
                to_feature_major(xn, TOK, xn_done, n0=c.n.get("xn", 0))
                c.tick("xn", TOK)
                slot("feat")
                slot("feat")
                slot("tok")
                slot("tok")
                s = wait_unit()
                pe.wait_ge(poollo_done, KT * (l + 1))
                for t in range(TOK):
                    for gp in range(2):
                        b = 4 + (2 * t + gp) % 4
                        take(b)
                        for g in (2 * gp, 2 * gp + 1):
                            o = bank[b][:, (g % 2) * 256:(g % 2) * 256 + 256]
                            for kk in range(2):
                                k, w0 = 2 * g + kk, (2 * g + kk) * 256
                                last = product(o, poolhi[:, k, t * P:t * P + P], poollo[:, k, t * P:t * P + P],
                                               whi[:, s, w0:w0 + 256], wlo[:, s, w0:w0 + 256], kk == 0, kk == 1)
                        last.then_inc(bank_full[b], 1)
                c.full(7, c.uses[7])

                def qk_turns(i):
                    def hook(t):
                        z = 4 * i + t
                        v = qy[:, z % 2, :]
                        head_turns(c.n.get("rope", 0) + z, t, [v[:, j * P:j * P + P] for j in range(4)], rope_done)
                    return hook

                slot("tok")
                slot("tok", qk_turns(0))
                slot("tok", qk_turns(1))
                slot("tok", qk_turns(2))
                slot("tok", qk_turns(3))
                slot("tok")
                c.tick("rope", 16)
                slot("tok")
                slot("tok")

                pe.wait_ge(s_const, 16 * 4)

                def logits(j):
                    h, i = ATT1[j]
                    w = (i + 1) * P
                    for comp in range(2):
                        b = 2 * (j % 2) + comp
                        take(b)
                        hc = 2 * h + comp
                        nc.tensor.matmul(bank[b][:, 0:w], qT[:, hc, i * P:i * P + P], kT[:, hc, 0:w],
                                         start=True, stop=False)
                        nc.tensor.matmul(bank[b][:, w - P:w], ident[:, :], chunkm[:, :],
                                         start=False, stop=True).then_inc(bank_full[b], 1)

                def turn(j):
                    h, i = ATT1[j]
                    b = 4 + j % 2
                    take(b)
                    pe.wait_ge(mixed, c.n.get("mixed", 0) + j + 1)
                    for kb in range(i + 1):
                        last = nc.tensor.transpose(bank[b][:, kb * P:kb * P + P], p1[:, j % 2, 0, kb * P:kb * P + P],
                                                   ident[:, :])
                    last.then_inc(bank_full[b], 1)

                def values(j):
                    h, i = ATT1[j]
                    b = 6 + j % 2
                    take(b)
                    tb = 4 + j % 2
                    pe.wait_ge(bank_free[tb], c.uses[tb])
                    for kb in range(i + 1):
                        last = nc.tensor.matmul(bank[b][:, 0:VD1], pt1[:, j % 2, kb * P:kb * P + P],
                                                v1[:, kb, h * VD1:h * VD1 + VD1], start=kb == 0, stop=kb == i)
                    last.then_inc(bank_full[b], 1)

                for b in range(8):
                    pe.wait_ge(bank_free[b], c.uses[b])
                logits(0)
                logits(1)
                for j in range(len(ATT1)):
                    if j + 2 < len(ATT1):
                        logits(j + 2)
                    turn(j)
                    if j:
                        values(j - 1)
                values(j)
                c.tick("mixed", len(ATT1))

                to_feature_major(M, TOK, m_done, n0=TOK * l)
                slot("tok")
                slot("tok")

                to_feature_major(xn, TOK, xn_done, n0=c.n["xn"])
                c.tick("xn", TOK)
                groups(GROUPS1)

            to_feature_major(xn, TOK, xn_done, n0=c.n["xn"])
            c.tick("xn", TOK)

            def pair_turns(a, pairs):
                def hook(t):
                    v = rot[:, t % 2, 0, :]
                    head_turns(a + t, t, [pairs(v, j) for j in range(4)], rope_done)
                return hook

            def plain_pair(v, j):
                return v[:, j * P:j * P + P]

            def indexer_turns(a):
                return lambda t: head_turns(a + t, t, [rot[:, t % 2, int(j < 2), j * P:j * P + P] for j in range(4)],
                                            rope_done)

            def attention(items, q, k, v, span, vw, maxed):
                def logits(j):
                    h, i = items[j]
                    b = j % 4
                    take(b)
                    k0, w = span(i)
                    nc.tensor.matmul(bank[b][:, 0:w], q(h, i), k(h, k0, w), start=True, stop=True)\
                        .then_inc(bank_full[b], 1)

                def turn(j):
                    h, i = items[j]
                    b = 4 + j % 2
                    take(b)
                    pe.wait_ge(exp_done, maxed + j + 1)
                    k0, w = span(i)
                    for kb in range(w // P):
                        last = nc.tensor.transpose(bank[b][:, kb * P:kb * P + P], p2[:, j % 2, kb * P:kb * P + P],
                                                   ident[:, :])
                    last.then_inc(bank_full[b], 1)

                def values(j):
                    h, i = items[j]
                    b = 6 + j % 2
                    take(b)
                    tb = 4 + j % 2
                    pe.wait_ge(bank_free[tb], c.uses[tb])
                    k0, w = span(i)
                    for kb in range(w // P):
                        last = nc.tensor.matmul(bank[b][:, 0:vw], pt2[:, j % 2, kb * P:kb * P + P],
                                                v(h, k0 // P + kb), start=kb == 0, stop=kb == w // P - 1)
                    last.then_inc(bank_full[b], 1)

                for b in range(8):
                    pe.wait_ge(bank_free[b], c.uses[b])
                for j in range(3):
                    logits(j)
                for j in range(len(items)):
                    if j + 3 < len(items):
                        logits(j + 3)
                    turn(j)
                    if j:
                        values(j - 1)
                values(j)

            def lane(t, h, j, c0, w):
                r = DH2 * (h % 2)
                return t[r:r + DH2, j, c0:c0 + w]

            def merge(b):
                for half in range(2):
                    slot("tok")
                    if half == 0:
                        to_feature_major(y2, TOK, y_done, chunks=4, n0=c.n.get("y", 0))
                        c.tick("y", TOK)
                    slot("tok", left=(yThi, yTlo), halves=1)

            for g in range(3):
                a = c.n["rope"]
                slot("tok")
                slot("tok", pair_turns(a, plain_pair))
                slot("tok", pair_turns(a + TOK, plain_pair), tokens=lambda j: dil_cols(g, j * P, P))
                c.tick("rope", 2 * TOK)

                def head(t, h, c0, w):
                    rows = DH2 * (h % 2)
                    return t[rows:rows + DH2, h // 2, dil_cols(g, c0, w)]

                attention(DIL, lambda h, i: head(bq, h, i * P, P), lambda h, k0, w: head(bk, h, k0, w),
                          lambda h, kb: bv[:, kb, h * DH2:h * DH2 + DH2], lambda i: dil_span(g, i), DH2,
                          c.n.get("exp", 0))
                c.tick("exp", len(DIL))
            merge(1)

            a = c.n["rope"]
            slot("tok")
            slot("tok", indexer_turns(a), width=68, halves=1)

            def ik_turns(t):
                head_turns(a + TOK + t, t, [rot[:, t % 2, 1, 0:P]], rope_done)

            slot("tok", ik_turns)
            for t in range(TOK):
                pair_turns(a + 2 * TOK, plain_pair)(t)
            c.tick("rope", 3 * TOK)
            for b in range(8):
                pe.wait_ge(bank_free[b], c.uses[b])
            for i in range(1, TOK):
                for h in range(4):
                    take(h)
                    nc.tensor.matmul(bank[h][:, 0:(i + 1) * P], lane(iqT, h, h // 2, i * P, P),
                                     ik[DH2 * (h % 2):DH2 * (h % 2) + DH2, 0:(i + 1) * P], start=True, stop=True)\
                        .then_inc(bank_full[h], 1)
            attention(SELA, lambda h, i: lane(aq, h, h // 2, i * P, P), lambda h, k0, w: lane(ak, h, h // 4, k0, w),
                      lambda h, kb: av[:, kb, (h // 4) * DH2:(h // 4) * DH2 + DH2], lambda i: (0, (i + 1) * P), DH2,
                      c.n["exp"])
            c.tick("exp", len(SELA))
            merge(0)

            slot("feat")
            to_feature_major(memx, 2, xn_done, n0=c.n["xn"])
            c.tick("xn", 2)
            slot("feat", left=(memhi, memlo), n=MEM)
            slot("tok", left=(memhi, memlo), tiles=2)
            attention(MEMA, lambda h, i: mqT[:, h, i * P:i * P + P], lambda h, k0, w: km[:, h, k0:k0 + w],
                      lambda h, kb: vm[:, kb, h * P:h * P + P], lambda i: (0, MEM), P, c.n["exp"])
            c.tick("exp", len(MEMA))
            merge(2)

            pe.wait_ge(stage, 6)
            to_feature_major(merged, TOK, None)
            slot("tok")
            slot("tok")

            to_feature_major(xn, TOK, xn_done, n0=c.n["xn"])
            pe.wait_ge(wr_lo, 1)
            take(0)
            for k in range(KT):
                wait_left(k)
                last = product(bank[0][0:ROUTES, :], wrhi[:, k, :], wrlo[:, k, :], nThi[:, k, :], nTlo[:, k, :],
                               k == 0, k == KT - 1)
            last.then_inc(bank_full[0], 1)
            for t in range(TOK):
                take(t)
                nc.tensor.transpose(bank[t][:, 0:ROUTES], routeT[:, t * P:t * P + P], ident[0:ROUTES, 0:ROUTES])\
                    .then_inc(bank_full[t], 1)
            pe.wait_ge(member, 1)
            pe.wait_ge(s_tables, 16 * 3)
            pe.wait_ge(ones_done, 1)
            members = ep[:, 2, :, :].rearrange("p t e -> p (t e)")
            for b, weights in enumerate((tri, ones)):
                take(b)
                nc.tensor.matmul(bank[b][:, 0:TOK * EXPERTS], weights[:, :], members, start=True, stop=True)\
                    .then_inc(bank_full[b], 1)

            u, U = list(c.uses), c.unit

            def free(b, n):
                pe.wait_ge(bank_free[b], u[b] + n)

            def gather(i, n):
                pe.wait_ge(hot_done, i + 1)
                for k in range(KT):
                    b = 2 + k // 4
                    if k % 4 == 0:
                        free(b, n - 1)
                    for t in range(TOK):
                        last = nc.tensor.matmul(bank[b][:, (k % 4) * P:(k % 4) * P + P], xn[:, t, k * P:k * P + P],
                                                hot[:, t, :], start=t == 0, stop=t == TOK - 1)
                    if k % 4 == 3:
                        last.then_inc(bank_full[b], 1)

            def turn_hot(i):
                free(5, i)
                for t in range(TOK):
                    last = nc.tensor.transpose(bank[5][:, t * P:t * P + P], hot[:, t, :], ident[:, :])
                last.then_inc(bank_full[5], 1)

            def into(i, n):
                for b in (2, 3):
                    free(b, n)
                for j in range(4):
                    hi, lo = parts(U, j)
                    pe.wait_ge(split_done, U + 6 * i + j + 1)
                    b = j // 2
                    if j % 2 == 0:
                        free(b, i)
                    for kk in range(4):
                        k = 4 * (j % 2) + kk
                        last = product(bank[b][:, :], xghi[:, k, :], xglo[:, k, :],
                                       hi[:, kk * 512:kk * 512 + 512], lo[:, kk * 512:kk * 512 + 512],
                                       k == 0, k == KT - 1)
                    last.then_inc(bank_full[b] if j % 2 else first_half, 1)

            def scatter(i):
                free(7, i)
                free(5, i)
                for j in range(8):
                    t, half, b = j // 2, j % 2, 2 + j % 3
                    free(b, (3 * i - 2 if b == 4 else 4 * i - 2) + j // 3)
                    cs = slice(half * 512, half * 512 + 512)
                    nc.tensor.matmul(bank[b][:, :], hotT[:, t * P:t * P + P], yhi[:, cs], start=True, stop=False)
                    nc.tensor.matmul(bank[b][:, :], hotT[:, t * P:t * P + P], ylo[:, cs], start=False, stop=True)\
                        .then_inc(bank_full[b], 1)

            def turn_hidden(i):
                free(1, i + 1)
                free(4, 3 * i)
                for f in range(4):
                    last = nc.tensor.transpose(bank[4][:, f * P:f * P + P], mh[:, f * P:f * P + P], ident[:, :])
                last.then_inc(bank_full[4], 1)

            def outof(i):
                free(4, 3 * i + 1)
                for j in range(2):
                    hi, lo = parts(U, 4 + j)
                    pe.wait_ge(split_done, U + 6 * i + 5 + j)
                    for half in range(2):
                        b = 6 + half
                        if j == 0:
                            free(b, i)
                        for ff in range(2):
                            f, w0 = 2 * j + ff, ff * D + half * 512
                            last = product(bank[b][:, :], hthi[:, f, :], htlo[:, f, :], hi[:, w0:w0 + 512],
                                           lo[:, w0:w0 + 512], f == 0, f == 3)
                        if j:
                            last.then_inc(bank_full[b], 1)
                        elif half:
                            last.then_inc(first_half, 1)

            pe.wait_ge(placed, 1)
            chunks = pe.value_load(ids[0:1, CHUNKS:CHUNKS + 1], min_val=SEQ * 2 // P, max_val=CHUNKS - 1)
            gather(0, 1)
            turn_hot(0)
            into(0, 1)
            turn_hidden(0)
            gather(1, 2)
            outof(0)
            with pe.Fori(1, chunks) as i:
                turn_hot(i)
                into(i, 4 * i - 2)
                scatter(i)
                turn_hidden(i)
                gather(i + 1, 4 * i + 2)
                outof(i)
            scatter(chunks)

        @block.scalar
        def _(act):
            c = Ledger()

            def hi_part(s, width=UNIT):
                return nc.scalar.activation(whi[:, s, 0:width], raw[:, s, 0:width], ACT.Copy)

            def split_to(u):
                while c.split < min(u, STATIC_UNITS):
                    v = c.split
                    act.wait_ge(raw_full[v % RING], 32 * (v // RING + 1))
                    if v >= RING:
                        act.wait_ge(*c.released[v - RING])
                    hi_part(v % RING, 8 * 68 if v == NARROW_UNIT else UNIT).then_inc(hi_done, 1)
                    c.split += 1

            def norm_roots(src, tiles, junk, ready):
                for t in range(tiles):
                    act.wait_ge(*ready[t])
                    if t >= 2:
                        act.wait_ge(sq_done, c.n.get("sq", 0) + t - 1)
                    nc.scalar.activation(junk(t), src[:, t, :], ACT.Square, accum_out=stat[:, 0, t:t + 1])\
                        .then_inc(sq_done, 1)
                c.tick("sq", tiles)
                act.wait_ge(ms_done, c.tick("ms"))
                nc.scalar.activation(stat[:, 0, 0:tiles], stat[:, 1, 0:tiles], ACT.Sqrt).then_inc(root_done, 1)

            def left_hi(hi, gain=None, chunks=KT, n=SEQ, order=in_order):
                for k in range(chunks):
                    b = 4 + k % 4
                    act.wait_ge(bank_full[b], c.take(b))
                    if gain is None:
                        ins = nc.scalar.activation(*order(hi[:, k, 0:n], bank[b][:, 0:n]), ACT.Copy)
                    else:
                        ins = nc.scalar.activation(hi[:, k, 0:n], bank[b][:, 0:n], ACT.Identity,
                                                   scale=gcol[:, gain, k:k + 1])
                    ins.then_inc(nhi_done, 1)

            def norm(gain):
                norm_roots(x, TOK, lambda t: xn[:, t % 2, :], c.x)
                act.wait_ge(s_first, 16 * 2)
                left_hi(nThi, gain)

            def evacuate(outs, func=ACT.Copy, tiles=4, halves=2, n=512, **more):
                uses = slot_uses(c, tiles, halves)
                split_to(c.unit + 2)
                for j in range(tiles):
                    act.wait_ge(bank_full[j], uses[j])
                    nc.scalar.activation(outs(j), bank[j][:, 0:n], func, **more).then_inc(bank_free[j], 1)
                split_to(c.unit + 3)

            def turned(outs):
                for t in range(TOK):
                    b = 4 + t
                    act.wait_ge(bank_full[b], c.take(b))
                    for dst, c0, w in outs(t):
                        ins = nc.scalar.activation(dst, bank[b][:, c0:c0 + w].rearrange("p (j n) -> p j n", n=P),
                                                   ACT.Copy)
                    ins.then_inc(bank_free[b], 1)

            def groups(n):
                w = groups_begin(c, n)

                def silu(g):
                    for j in range(2):
                        act.wait_ge(bank_full[j], w.uses[j] + g + 1)
                        act.wait_ge(bank_free[2 + j], w.uses[2 + j] + g)
                        nc.scalar.activation(sg[:, j, :], bank[j][:, :], ACT.Silu).then_inc(bank_free[j], 1)

                def hidden_hi(g):
                    act.wait_ge(bank_free[3], w.uses[3] + g + 1)
                    act.wait_ge(bank_full[7], w.uses[7] + 2 * g)
                    nc.scalar.activation(hhi[:, :, :], hf[:, :, :], ACT.Copy).then_inc(hhi_done, 1)

                def split_unit(u, s, turns, released):
                    act.wait_ge(raw_full[s], turns)
                    act.wait_ge(*released)
                    hi_part(s).then_inc(hi_done, 1)

                c.half()
                c.full(3, w.uses[3] + 1)
                split_to(w.unit + 4)
                silu(0)
                split_to(w.unit + 5)
                hidden_hi(0)

                def landed(r, g):
                    return 32 * ((w.unit + r) // RING + 1) + 32 * g

                def body(g):
                    s = [(w.unit + r) % RING for r in (5, 6, 7)]
                    split_unit(5, s[0], landed(5, g), (first_half, w.halves + g + 2))
                    silu(g + 1)
                    split_unit(6, s[1], landed(6, g), (bank_full[3], w.uses[3] + g + 2))
                    split_unit(7, s[2], landed(7, g), (bank_full[7], w.uses[7] + 2 * g + 2))
                    hidden_hi(g + 1)

                with act.Fori(0, n - 1) as g:
                    body(g)
                c.halves, c.unit, c.released[w.unit:] = w.halves, w.unit, []
                groups_end(c, w)
                c.split = min(w.unit + 3 * n + 2, STATIC_UNITS)

            for l in range(LAYERS):
                norm(2 * l)
                act.wait_ge(s_const, 16 * 4)
                for _ in range(2):
                    uses = slot_uses(c)
                    split_to(c.unit + 2)
                    for j in range(4):
                        m = c.tick("u")
                        act.wait_ge(bank_full[j], uses[j])
                        if m == 1 or (m - 1) % KT == 0:
                            act.wait_ge(pad_zero, l + 1)
                        nc.scalar.activation(win[:, m % 2, 16:16 + SEQ], bank[j][:, :], ACT.Copy)\
                            .then_inc(bank_free[j], 1)
                        act.wait_ge(pooled, m)
                        nc.scalar.activation(poolhi[:, (m - 1) % KT, :], win[:, 2, 16:16 + SEQ], ACT.Copy)\
                            .then_inc(poolhi_done, 1)
                    split_to(c.unit + 3)
                for half in range(2):
                    evacuate(lambda j: M[:, j, half * 512:half * 512 + 512], ACT.Sigmoid)
                for k in range(8):
                    c.take(4 + k % 4)
                c.full(7, c.uses[7])
                for i in range(4):
                    uses = slot_uses(c)
                    split_to(c.unit + 2)
                    for t in range(TOK):
                        z = c.tick("qk")
                        act.wait_ge(bank_full[t], uses[t])
                        if z > 1:
                            act.wait_ge(qms_done, z - 1)
                        nc.scalar.activation(qsq[:, :], bank[t][:, :], ACT.Square).then_inc(qsq_done, 1)
                        act.wait_ge(qms_done, z)
                        nc.scalar.activation(qst[:, 0, :], qst[:, 1, :], ACT.Sqrt).then_inc(qroot_done, 1)
                    split_to(c.unit + 3)
                    dst = (qT, kT)[i // 2]
                    turned(lambda t: [(dst[:, 4 * (i % 2):4 * (i % 2) + 4, t * P:t * P + P], 0, 512)])
                for half in range(2):
                    evacuate(lambda j: v1[:, j, half * 512:half * 512 + 512])
                for half in range(2):
                    evacuate(lambda j: G[:, j, half * 512:half * 512 + 512], ACT.Sigmoid)
                act.wait_ge(lam_dot, l + 1)
                nc.scalar.activation(lams[:, 2:4], lams[:, 0:2], ACT.Exp).then_inc(lam_exp, 1)

                j0 = c.n.get("neg", 0)
                uses = []
                for j in range(len(ATT1)):
                    bs = (2 * (j % 2), 2 * (j % 2) + 1, 4 + j % 2, 6 + j % 2)
                    uses.append([(b, c.take(b)) for b in bs])

                def exps(j):
                    h, i = ATT1[j]
                    w = (i + 1) * P
                    act.wait_ge(negmax, j0 + j + 1)
                    for comp in range(2):
                        b, n = uses[j][comp]
                        if j >= 2:
                            tb, tn = uses[j - 2][2]
                            act.wait_ge(bank_full[tb], tn)
                        nc.scalar.activation(p1[:, j % 2, comp, 0:w], bank[b][:, 0:w], ACT.Exp, scale=SCALE1,
                                             bias=ast1[:, 2 + comp, j:j + 1], accum_out=ast1[:, 4 + comp, j:j + 1])\
                            .then_inc(bank_free[b], 1)

                def turned_weights(j):
                    w = (ATT1[j][1] + 1) * P
                    b, n = uses[j][2]
                    act.wait_ge(bank_full[b], n)
                    if j >= 2:
                        act.wait_ge(bank_full[uses[j - 2][3][0]], uses[j - 2][3][1])
                    nc.scalar.activation(pt1[:, j % 2, 0:w], bank[b][:, 0:w], ACT.Copy).then_inc(bank_free[b], 1)

                def result(j):
                    b, n = uses[j][3]
                    act.wait_ge(bank_full[b], n)
                    if j >= 2:
                        act.wait_ge(bank_free[b], n - 1)
                    scratch = lvec[:, 2 * (j % 2):2 * (j % 2) + 2, :].rearrange("p a b -> p (a b)")
                    nc.scalar.activation(scratch, bank[b][:, 0:VD1], ACT.Square,
                                         scale=ast1[:, 6, j:j + 1], accum_out=ast1[:, 7, j:j + 1])
                    nc.scalar.activation(oall[:, j, :], bank[b][:, 0:VD1], ACT.Identity, scale=ast1[:, 6, j:j + 1])\
                        .then_inc(bank_free[b], 1)

                for j in range(len(ATT1) + 2):
                    if j < len(ATT1):
                        exps(j)
                    if 1 <= j <= len(ATT1):
                        turned_weights(j - 1)
                    if j >= 2:
                        result(j - 2)
                c.tick("neg", len(ATT1))
                act.wait_ge(ms_done, c.tick("ms"))
                nc.scalar.activation(ast1[:, 8, :], ast1[:, 7, :], ACT.Sqrt).then_inc(root_done, 1)

                left_hi(nThi)
                slot_uses(c)
                split_to(c.unit + 3)
                uses = slot_uses(c)
                split_to(c.unit + 3)
                c.x = [(bank_free[t], uses[t]) for t in range(TOK)]
                norm(2 * l + 1)
                groups(GROUPS1)

            norm(2 * LAYERS)

            def attention(items, span, vw, outs, masked, scale):
                uses = []
                for j in range(len(items)):
                    uses.append([(b, c.take(b)) for b in (j % 4, 4 + j % 2, 6 + j % 2)])

                def exps(j):
                    w = span(items[j][1])[1]
                    act.wait_ge(negmax, c.n["neg"] + j + 1)
                    src = p2[:, j % 2, 0:w] if masked else bank[j % 4][:, 0:w]
                    if not masked and j >= 2:
                        act.wait_ge(bank_full[uses[j - 2][1][0]], uses[j - 2][1][1])
                    nc.scalar.activation(p2[:, j % 2, 0:w], src, ACT.Exp, scale=scale,
                                         bias=ast2[:, 1, outs(j):outs(j) + 1],
                                         accum_out=ast2[:, 2, outs(j):outs(j) + 1]).then_inc(exp_done, 1)

                def turned_weights(j):
                    w = span(items[j][1])[1]
                    b, n = uses[j][1]
                    act.wait_ge(bank_full[b], n)
                    if j >= 2:
                        act.wait_ge(bank_full[uses[j - 2][2][0]], uses[j - 2][2][1])
                    nc.scalar.activation(pt2[:, j % 2, 0:w], bank[b][:, 0:w], ACT.Copy).then_inc(bank_free[b], 1)

                for j in range(len(items) + 1):
                    if j < len(items):
                        exps(j)
                    if j:
                        turned_weights(j - 1)
                c.tick("neg", len(items))
                c.tick("exp", len(items))

            def merge(b):
                for half in range(2):
                    slot_uses(c)
                    split_to(c.unit + 2)
                    if half == 0:
                        left_hi(yThi, chunks=4, order=from_residues if b == 1 else in_order)
                    for t in range(TOK):
                        act.wait_ge(bank_free[t], c.uses[t])
                        nc.scalar.activation(gbuf[:, t, :], gbuf[:, t, :], ACT.Sigmoid).then_inc(sig_done, 1)
                    split_to(c.unit + 3)
                    slot_uses(c, halves=1)
                    split_to(c.unit + 2)

            def pairs_to(dst):
                turned(lambda t: [(dst[:, :, t * P:t * P + P], 0, 512)])

            for g in range(3):
                for dst in (bq, bk):
                    slot_uses(c)
                    split_to(c.unit + 3)
                    pairs_to(dst)
                evacuate(lambda j: bv[:, j, :])
                attention(DIL, lambda i: dil_span(g, i), DH2,
                          lambda j: g * 32 + DIL[j][1] * 8 + DIL[j][0], True, SCALE2)
            act.wait_ge(shifted, 1)
            nc.scalar.activation(ast2[:, 4, :], ast2[:, 3, :], ACT.Exp, scale=SCALE2).then_inc(raised, 1)
            merge(1)

            uses = slot_uses(c)
            split_to(c.unit + 2)
            for t in range(TOK):
                act.wait_ge(bank_full[t], uses[t])
                nc.scalar.activation(av[:, t, :], bank[t][:, 128:256], ACT.Copy).then_inc(side_done, 1)
            split_to(c.unit + 3)
            turned(lambda t: [(ak[:, :, t * P:t * P + P], 0, 256), (iqT[:, :, t * P:t * P + P], 256, 256)])
            uses = slot_uses(c, halves=1)
            split_to(c.unit + 2)
            for t in range(TOK):
                act.wait_ge(bank_full[t], uses[t])
                nc.scalar.activation(iw[:, t, :], bank[t][:, 64:68], ACT.Copy, scale=0.5).then_inc(side_done, 1)
            split_to(c.unit + 3)
            turned(lambda t: [(ik[:, t * P:t * P + P].unsqueeze(1), 0, 128)])
            slot_uses(c)
            split_to(c.unit + 3)
            pairs_to(aq)
            n = 0
            for i in range(1, TOK):
                for h in range(4):
                    act.wait_ge(bank_full[h], c.take(h))
                    if n >= 2:
                        act.wait_ge(relu_used, n - 1)
                    nc.scalar.activation(relu[:, h % 2, 0:(i + 1) * P], bank[h][:, 0:(i + 1) * P], ACT.Relu,
                                         scale=0.125).then_inc(bank_free[h], 1)
                    n += 1
            attention(SELA, lambda i: (0, (i + 1) * P), DH2, lambda j: j, True, SCALE2)
            merge(0)

            norm_roots(memx, 2, lambda t: memj[:, t, :], [(s_mem, 16)] * 2)
            evacuate(lambda j: mqT[:, j, :])
            left_hi(memhi, 2 * LAYERS + 2, n=MEM)
            evacuate(lambda j: km[:, j, :], n=MEM)
            evacuate(lambda j: vm[:, j, :], tiles=2)
            attention(MEMA, lambda i: (0, MEM), P, lambda j: j, False, SCALE_M)
            merge(2)
            left_hi(nThi)
            slot_uses(c)
            split_to(c.unit + 3)
            uses = slot_uses(c)
            split_to(c.unit + 3)
            c.x = [(bank_free[t], uses[t]) for t in range(TOK)]

            act.wait_ge(s_route, 16 * 7)
            nc.scalar.activation(wrhi[:, :, :], wr[:, :, :], ACT.Copy).then_inc(wr_hi, 1)
            norm(2 * LAYERS + 1)
            act.wait_ge(bank_full[0], c.take(0))
            nc.scalar.activation(routeT[:, :], bank[0][0:ROUTES, :], ACT.Copy).then_inc(bank_free[0], 1)
            for t in range(TOK):
                c.take(t)
            act.wait_ge(shifted, 2)
            nc.scalar.activation(rt[:, 1, :, :], rt[:, 0, :, :], ACT.Exp).then_inc(raised, 1)
            act.wait_ge(shifted, 3)
            nc.scalar.activation(rt[:, 9, :, 0:1], rt[:, 8, :, 0:1], ACT.Exp).then_inc(raised, 1)
            routed = (bank_full[3], c.uses[3])
            for b in range(2):
                c.take(b)
            act.wait_ge(placed, 1)
            chunks = nc.scalar.value_load(ids[0:1, CHUNKS:CHUNKS + 1], min_val=SEQ * 2 // P, max_val=CHUNKS - 1)
            u, U, F = list(c.uses), c.unit, c.halves

            def full(b, n):
                act.wait_ge(bank_full[b], u[b] + n)

            def split_unit(i, j, release=None):
                s = (U + j) % RING
                act.wait_ge(raw_full[s], 32 * ((U + j) // RING + 1) + 64 * i)
                if release:
                    act.wait_ge(*release)
                nc.scalar.activation(parts(U, j)[0], raw[:, s, :], ACT.Copy).then_inc(hi_done, 1)

            def gathered(n, banks=(2, 3)):
                for b in banks:
                    full(b, n)
                    for k in range(4 * (b - 2), 4 * (b - 2) + 4):
                        hi = nc.scalar.activation(xghi[:, k, :], bank[b][:, (k % 4) * P:(k % 4) * P + P],
                                                  ACT.Identity, scale=gcol[:, 2 * LAYERS + 1, k:k + 1])
                    hi.then_inc(nhi_done, 1)

            def chunk(i):
                first = isinstance(i, int)
                split_unit(i, 5, None if first else (bank_full[7], u[7] + i))
                split_unit(i, 6, (first_half, F + 3 * i + 1))
                full(0, i + 1)
                nc.scalar.activation(msg[:, :], bank[0][:, :], ACT.Silu).then_inc(bank_free[0], 1)
                split_unit(i, 7, (bank_full[0], u[0] + i + 1))
                split_unit(i, 8, (first_half, F + 3 * i + 2))
                full(5, i + 1)
                if not isinstance(i, int):
                    full(3, 4 * i + 1)
                nc.scalar.activation(hotT[:, :], bank[5][:, :], ACT.Copy).then_inc(bank_free[5], 1)
                full(4, 3 * i + 1)
                nc.scalar.activation(hthi[:, :, :].rearrange("p k n -> p (k n)"), bank[4][:, :], ACT.Copy)\
                    .then_inc(ht_hi, 1)
                gathered(4 * i + 2, (2,))
                split_unit(i, 9, (bank_full[1], u[1] + i + 1))
                gathered(4 * i + 2, (3,))
                split_unit(i, 10, (first_half, F + 3 * i + 3))
                for b in (6, 7):
                    full(b, i + 1)
                    nc.scalar.activation(yhi[:, (b - 6) * 512:(b - 6) * 512 + 512], bank[b][:, :], ACT.Copy)\
                        .then_inc(y_hi, 1)

            split_unit(0, 0, c.released[U - 3])
            split_unit(0, 1, c.released[U - 2])
            gathered(1)
            split_unit(0, 2, c.released[U - 1])
            split_unit(0, 3, routed)
            split_unit(0, 4, routed)
            chunk(0)
            with act.Fori(1, chunks) as i:
                chunk(i)

            norm_roots(x, TOK, lambda t: xn[:, t, :], [(x_final, 1)] * TOK)

        @block.vector
        def _(dve):
            c = Ledger()
            v = nc.vector

            def note(ins):
                ins.then_inc(chain, c.tick("chain") and 1)

            def settle():
                dve.wait_ge(chain, c.n["chain"])

            def link(ins):
                note(ins)
                settle()

            def lo_part(s, width=UNIT):
                return v.tensor_tensor(wlo[:, s, 0:width], raw[:, s, 0:width], whi[:, s, 0:width].bitcast(F32),
                                       ALU.subtract)

            def split_to(u):
                while c.split < min(u, STATIC_UNITS):
                    w = c.split
                    dve.wait_ge(hi_done, w + 1)
                    lo_part(w % RING, 8 * 68 if w == NARROW_UNIT else UNIT).then_inc(split_done, 1)
                    c.split += 1

            def mean_roots(tiles, width):
                dve.wait_ge(sq_done, c.tick("sq", tiles))
                v.tensor_scalar(stat[:, 1, 0:tiles], stat[:, 0, 0:tiles], 1.0 / width, EPS, ALU.mult, ALU.add)\
                    .then_inc(ms_done, 1)
                dve.wait_ge(root_done, c.tick("root"))
                link(v.reciprocal(stat[:, 2, 0:tiles], stat[:, 0, 0:tiles]))

            def left_lo(hi, lo, gain=None, chunks=KT, n=SEQ, order=in_order):
                for k in range(chunks):
                    b = 4 + k % 4
                    c.take(b)
                    dve.wait_ge(nhi_done, c.tick("nhi"))
                    top = hi[:, k, 0:n].bitcast(F32)
                    if gain is None:
                        ins = v.tensor_tensor(*order(lo[:, k, 0:n], bank[b][:, 0:n]), order(top, bank[b][:, 0:n])[0],
                                              ALU.subtract)
                    else:
                        ins = v.scalar_tensor_tensor(out=lo[:, k, 0:n], in0=bank[b][:, 0:n],
                                                     scalar=gcol[:, gain, k:k + 1], in1=top,
                                                     op0=ALU.mult, op1=ALU.subtract)
                    ins.then_inc(bank_free[b], 1)

            def norm(gain):
                mean_roots(TOK, D)
                for t in range(TOK):
                    v.tensor_scalar(xn[:, t, :], x[:, t, :], stat[:, 2, t:t + 1], None, ALU.mult).then_inc(xn_done, 1)
                dve.wait_ge(s_first, 16 * 2)
                left_lo(nThi, nTlo, gain)

            def add_to_x(half):
                uses = slot_uses(c)
                split_to(c.unit + 2)
                for t in range(TOK):
                    dve.wait_ge(bank_full[t], uses[t])
                    xs = x[:, t, half * 512:half * 512 + 512]
                    v.tensor_tensor(xs, bank[t][:, :], xs, ALU.add).then_inc(bank_free[t], 1)
                split_to(c.unit + 3)
                c.x = [(bank_free[t], uses[t]) for t in range(TOK)]

            def groups(n):
                w = groups_begin(c, n)

                def hidden(g):
                    for j in range(2):
                        dve.wait_ge(bank_free[j], w.uses[j] + g + 1)
                        dve.wait_ge(bank_full[2 + j], w.uses[2 + j] + g + 1)
                        if j == 0 and (w.h or not isinstance(g, int)):
                            dve.wait_ge(hlo_done, w.h + g)
                        v.tensor_tensor(hf[:, j, :], bank[2 + j][:, :], sg[:, j, :], ALU.mult)\
                            .then_inc(bank_free[2 + j], 1)

                def hidden_lo(g):
                    dve.wait_ge(hhi_done, w.h + g + 1)
                    v.tensor_tensor(hlo[:, :, :], hf[:, :, :], hhi[:, :, :].bitcast(F32), ALU.subtract)\
                        .then_inc(hlo_done, 1)

                def outof(g):
                    dve.wait_ge(bank_free[7], w.uses[7] + 2 * g)
                    for tile in range(8):
                        t, half, b = tile // 2, tile % 2, 4 + tile % 4
                        dve.wait_ge(bank_full[b], w.uses[b] + 2 * g + tile // 4 + 1)
                        xs = x[:, t, half * 512:half * 512 + 512]
                        v.tensor_tensor(xs, bank[b][:, :], xs, ALU.add).then_inc(bank_free[b], 1)

                def split_unit(r, g):
                    u = w.unit + r + 3 * g
                    dve.wait_ge(hi_done, u + 1)
                    lo_part((w.unit + r) % RING).then_inc(split_done, 1)

                c.half()
                c.full(3, w.uses[3] + 1)
                split_to(w.unit + 4)
                hidden(0)
                split_to(w.unit + 5)
                hidden_lo(0)
                with dve.Fori(0, n - 1) as g:
                    split_unit(5, g)
                    hidden(g + 1)
                    split_unit(6, g)
                    outof(g)
                    split_unit(7, g)
                    hidden_lo(g + 1)
                outof(n - 1)
                c.halves, c.unit, c.released[w.unit:] = w.halves, w.unit, []
                groups_end(c, w)
                c.split = min(w.unit + 3 * n + 2, STATIC_UNITS)

            dve.wait_ge(*c.x[-1])
            for l in range(LAYERS):
                norm(2 * l)
                dve.wait_ge(s_const, 16 * 4)
                v.memset(win[:, :, 0:16], 0.0).then_inc(pad_zero, 1)
                dve.wait_ge(pad_zero, l + 1)
                for _ in range(2):
                    uses = slot_uses(c)
                    split_to(c.unit + 2)
                    for j in range(4):
                        m = c.tick("u")
                        g = (m - 1) % KT // 2
                        dve.wait_ge(bank_free[j], uses[j])
                        here, at_ = win[:, m % 2, :], 3
                        for level in range(g + 1):
                            link(v.tensor_tensor(win[:, at_, 16:16 + SEQ], here[:, 16:16 + SEQ],
                                                 here[:, 16 - 2 ** level:16 + SEQ - 2 ** level], ALU.add))
                            here, at_ = win[:, at_, :], 5 - at_
                        u = win[:, m % 2, :]
                        link(v.tensor_tensor(qst16[:, :], here[:, 16:32], countw[:, g, :], ALU.mult))
                        link(v.scalar_tensor_tensor(out=win[:, 2, 32:16 + SEQ], in0=here[:, 32:16 + SEQ],
                                                    scalar=1.0 / POOL_WINDOWS[g], in1=u[:, 32:16 + SEQ],
                                                    op0=ALU.mult, op1=ALU.subtract))
                        v.tensor_tensor(win[:, 2, 16:32], qst16[:, :], u[:, 16:32], ALU.subtract).then_inc(pooled, 1)
                        dve.wait_ge(poolhi_done, m)
                        v.tensor_tensor(poollo[:, (m - 1) % KT, :], win[:, 2, 16:16 + SEQ],
                                        poolhi[:, (m - 1) % KT, :].bitcast(F32), ALU.subtract).then_inc(poollo_done, 1)
                        dve.wait_ge(poollo_done, m)
                    split_to(c.unit + 3)
                dve.wait_ge(s_layer, 16 * 8 * (l + 1))
                for half in range(2):
                    uses = slot_uses(c)
                    split_to(c.unit + 2)
                    for t in range(TOK):
                        dve.wait_ge(bank_free[t], uses[t])
                        ms = M[:, t, half * 512:half * 512 + 512]
                        note(v.tensor_tensor(ms, ms, prow[:, half * 512:half * 512 + 512], ALU.mult))
                    split_to(c.unit + 3)
                settle()
                for k in range(8):
                    b = 4 + k % 4
                    dve.wait_ge(bank_full[b], c.take(b))
                    ms = M[:, k // 2, (k % 2) * 512:(k % 2) * 512 + 512]
                    v.tensor_tensor(ms, bank[b][:, :], ms, ALU.mult).then_inc(bank_free[b], 1)
                c.full(7, c.uses[7])

                zs = []
                for i in range(4):
                    uses = slot_uses(c)
                    split_to(c.unit + 2)
                    for t in range(TOK):
                        z = c.tick("qk")
                        y = qy[:, (z - 1) % 2, :].rearrange("p (j n) -> p j n", n=P)
                        dve.wait_ge(qsq_done, z)
                        link(v.tensor_reduce(qst[:, 2, :], qsq[:, :].rearrange("p (j n) -> p j n", n=P), AX.X, ALU.add))
                        v.tensor_scalar(qst[:, 1, :], qst[:, 2, :], 1.0 / DH1, EPS, ALU.mult, ALU.add)\
                            .then_inc(qms_done, 1)
                        dve.wait_ge(qroot_done, z)
                        link(v.reciprocal(qst[:, 2, :], qst[:, 0, :]))
                        if len(zs) >= 2:
                            dve.wait_ge(*zs[-2])
                        for j in range(4):
                            ins = v.scalar_tensor_tensor(out=y[:, j, :], in0=bank[t][:, j * P:j * P + P],
                                                         scalar=qst[:, 2, j:j + 1], in1=qkg[:, i // 2, :],
                                                         op0=ALU.mult, op1=ALU.mult)
                            if j < 3:
                                note(ins)
                        ins.then_inc(bank_free[t], 1)
                        dve.wait_ge(bank_free[t], uses[t])
                        cos = rope1[:, t, 0:ROT_HALF].unsqueeze(1).to_broadcast([P, 4, ROT_HALF])
                        sin = rope1[:, t, ROT_HALF:2 * ROT_HALF].unsqueeze(1).to_broadcast([P, 4, ROT_HALF])
                        y1, y2_ = y[:, :, 0:ROT_HALF], y[:, :, ROT_HALF:2 * ROT_HALF]
                        r = [qrot[:, k, :].rearrange("p (j n) -> p j n", n=ROT_HALF) for k in range(4)]
                        note(v.tensor_tensor(r[0], y1, cos, ALU.mult))
                        note(v.tensor_tensor(r[1], y2_, sin, ALU.mult))
                        note(v.tensor_tensor(r[2], y2_, cos, ALU.mult))
                        link(v.tensor_tensor(r[3], y1, sin, ALU.mult))
                        note(v.tensor_tensor(y1, r[0], r[1], ALU.subtract))
                        v.tensor_tensor(y2_, r[2], r[3], ALU.add).then_inc(rope_done, 1)
                        c.tick("rope")
                        zs.append((bank_full[4 + t], c.take(4 + t)))
                    split_to(c.unit + 3)
                for half in range(2):
                    slot_uses(c)
                    split_to(c.unit + 3)
                link(v.tensor_scalar(subg[:, :], subg[:, :], lamc[:, l, 1:2], None, ALU.mult))
                for half in range(2):
                    uses = slot_uses(c)
                    split_to(c.unit + 2)
                    for t in range(TOK):
                        dve.wait_ge(bank_free[t], uses[t])
                        gs = G[:, t, half * 512:half * 512 + 512].rearrange("p (a b) -> p a b", b=VD1)
                        note(v.tensor_tensor(gs, gs, subg[:, :].unsqueeze(1).to_broadcast([P, 2, VD1]), ALU.mult))
                    split_to(c.unit + 3)
                for j in range(2):
                    ins = v.tensor_tensor_reduce(out=lvec[:, 2 * j, :], in0=lvec[:, 2 * j, :], in1=lvec[:, 2 * j + 1, :],
                                                 scale=1.0, scalar=0.0, op0=ALU.mult, op1=ALU.add,
                                                 accum_out=lams[:, j:j + 1])
                    if j == 0:
                        note(ins)
                ins.then_inc(lam_dot, 1)
                dve.wait_ge(lam_exp, l + 1)
                link(v.tensor_tensor(lams[:, 0:1], lams[:, 3:4], lams[:, 2:3], ALU.subtract))
                link(v.tensor_tensor(lams[:, 0:1], lams[:, 0:1], lamc[:, l, 0:1], ALU.subtract))

                uses = []
                for j in range(len(ATT1)):
                    uses.append([(b, c.take(b)) for b in (2 * (j % 2), 2 * (j % 2) + 1, 4 + j % 2, 6 + j % 2)])

                def maxima(j):
                    w = (ATT1[j][1] + 1) * P
                    for comp in range(2):
                        b, n = uses[j][comp]
                        dve.wait_ge(bank_full[b], n)
                        ins = v.reduce_max(ast1[:, comp, j:j + 1], bank[b][:, 0:w], AX.X)
                        note(ins)
                    settle()
                    v.tensor_scalar(ast1[:, 2:4, j:j + 1], ast1[:, 0:2, j:j + 1], -SCALE1, None, ALU.mult)\
                        .then_inc(negmax, 1)

                def mix(j):
                    w = (ATT1[j][1] + 1) * P
                    for comp in range(2):
                        b, n = uses[j][comp]
                        dve.wait_ge(bank_free[b], n)
                    link(v.reciprocal(ast1[:, 9, j:j + 1], ast1[:, 5, j:j + 1]))
                    link(v.scalar_tensor_tensor(out=ast1[:, 9, j:j + 1], in0=ast1[:, 9, j:j + 1], scalar=lams[:, 0:1],
                                                in1=ast1[:, 4, j:j + 1], op0=ALU.mult, op1=ALU.mult))
                    note(v.reciprocal(ast1[:, 6, j:j + 1], ast1[:, 4, j:j + 1]))
                    v.scalar_tensor_tensor(out=p1[:, j % 2, 0, 0:w], in0=p1[:, j % 2, 1, 0:w],
                                           scalar=ast1[:, 9, j:j + 1], in1=p1[:, j % 2, 0, 0:w],
                                           op0=ALU.mult, op1=ALU.add).then_inc(mixed, 1)

                maxima(0)
                for j in range(len(ATT1)):
                    if j + 1 < len(ATT1):
                        maxima(j + 1)
                    mix(j)
                for b in (6, 7):
                    dve.wait_ge(bank_free[b], c.uses[b])
                v.tensor_scalar(ast1[:, 7, :], ast1[:, 7, :], 1.0 / VD1, EPS, ALU.mult, ALU.add).then_inc(ms_done, 1)
                dve.wait_ge(root_done, c.tick("root"))
                link(v.reciprocal(ast1[:, 9, :], ast1[:, 8, :]))
                for i in range(TOK):
                    for h in range(HEADS1):
                        j = h * TOK + i
                        note(v.scalar_tensor_tensor(out=oall[:, j, :], in0=oall[:, j, :], scalar=ast1[:, 9, j:j + 1],
                                                    in1=G[:, i, h * VD1:h * VD1 + VD1], op0=ALU.mult, op1=ALU.mult))
                    settle()
                    om = oall[:, i:i + 13:TOK, :]
                    mm = M[:, i, :].rearrange("p (h n) -> p h n", n=VD1)
                    v.tensor_tensor(mm, mm, om, ALU.add).then_inc(m_done, 1)
                dve.wait_ge(m_done, TOK * (l + 1))
                dve.drain().then_inc(mixer_done, 1)

                left_lo(nThi, nTlo)
                add_to_x(0)
                add_to_x(1)
                dve.wait_ge(*c.x[-1])
                norm(2 * l + 1)
                groups(GROUPS1)
                dve.wait_ge(*c.x[-1])

            norm(2 * LAYERS)

            def rotate(t, bt, n, doubled):
                heads = n // DH2
                a = rot[:, t % 2, 0, 0:n].rearrange("p (h d) -> p h d", d=DH2)
                b = rot[:, t % 2, 1, 0:n].rearrange("p (h d) -> p h d", d=DH2)
                src = bank[t][:, 0:n].rearrange("p (h d) -> p h d", d=DH2)
                half = DH2 // 2

                def row(c0, w):
                    return rope2[:, t, c0:c0 + w].unsqueeze(1).to_broadcast([P, heads, w])

                note(v.tensor_tensor(a, src, row(0, DH2), ALU.mult))
                note(v.tensor_tensor(b[:, :, 0:half], src[:, :, half:DH2], row(DH2, half), ALU.mult))
                v.tensor_tensor(b[:, :, half:DH2], src[:, :, 0:half], row(DH2 + half, half), ALU.mult)\
                    .then_inc(bank_free[t], 1)
                dve.wait_ge(bank_free[t], bt)
                if not doubled:
                    v.tensor_tensor(a, a, b, ALU.add).then_inc(rope_done, 1)
                else:
                    link(v.tensor_tensor(a, a, b, ALU.add))
                    two = rot[:, t % 2, 1, 0:doubled * P].rearrange("p (h c d) -> p h c d", c=2, d=DH2)
                    v.tensor_copy(two, a[:, 0:doubled, :].unsqueeze(2).to_broadcast([P, doubled, 2, DH2]))\
                        .then_inc(rope_done, 1)

            def rotated_slot(n=512, halves=2, side=False, doubled=0):
                uses = slot_uses(c, halves=halves)
                split_to(c.unit + 2)
                for t in range(TOK):
                    dve.wait_ge(bank_full[t], uses[t])
                    if side:
                        dve.wait_ge(side_done, c.tick("side"))
                    if len(c.turns) >= 2:
                        dve.wait_ge(*c.turns[-2])
                    rotate(t, uses[t], n, doubled)
                    c.turns.append((bank_full[4 + t], c.take(4 + t)))
                split_to(c.unit + 3)

            def attention(items, span, vw, outs, mask, scale, result, between=None):
                uses = []
                for j in range(len(items)):
                    uses.append([(b, c.take(b)) for b in (j % 4, 4 + j % 2, 6 + j % 2)])

                def maxima(j):
                    h, i = items[j]
                    w = span(i)[1]
                    o = outs(j)
                    b, n = uses[j][0]
                    dve.wait_ge(bank_full[b], n)
                    if mask is None:
                        link(v.reduce_max(ast2[:, 0, o:o + 1], bank[b][:, 0:w], AX.X))
                    else:
                        if j >= 2:
                            dve.wait_ge(bank_full[uses[j - 2][1][0]], uses[j - 2][1][1])
                        v.tensor_tensor_reduce(out=p2[:, j % 2, 0:w], in0=bank[b][:, 0:w], in1=mask(i, w), scale=1.0,
                                               scalar=PICKED, op0=ALU.add, op1=ALU.max,
                                               accum_out=ast2[:, 0, o:o + 1]).then_inc(bank_free[b], 1)
                        dve.wait_ge(bank_free[b], n)
                    v.tensor_scalar(ast2[:, 1, o:o + 1], ast2[:, 0, o:o + 1], -scale, None, ALU.mult)\
                        .then_inc(negmax, 1)

                def take_result(j):
                    b, n = uses[j][2]
                    dve.wait_ge(bank_full[b], n)
                    result(j, bank[b][:, 0:vw]).then_inc(bank_free[b], 1)

                maxima(0)
                for j in range(len(items)):
                    if between:
                        between(j)
                    if j + 1 < len(items):
                        maxima(j + 1)
                    if j:
                        take_result(j - 1)
                    if mask is None:
                        dve.wait_ge(exp_done, c.n.get("exp", 0) + j + 1)
                        dve.drain().then_inc(bank_free[uses[j][0][0]], 1)
                take_result(j)
                c.tick("exp", len(items))

            def divided(items, vw):
                def result(j, o):
                    h, i = items[j]
                    link(v.reciprocal(ast2[:, 3, j:j + 1], ast2[:, 2, j:j + 1]))
                    return v.tensor_scalar(y2[:, i, h * vw:h * vw + vw], o, ast2[:, 3, j:j + 1], None, ALU.mult)
                return result

            def milestone():
                dve.drain().then_inc(stage, 1)

            def merge(b):
                for half in range(2):
                    uses = slot_uses(c)
                    split_to(c.unit + 2)
                    dve.wait_ge(s_bg, 16 * c.tick("bg"))
                    for t in range(TOK):
                        dve.wait_ge(bank_full[t], uses[t])
                        v.tensor_tensor(gbuf[:, t, :], bank[t][:, :], bg[:, :], ALU.add).then_inc(bank_free[t], 1)
                    dve.wait_ge(bank_free[3], uses[3])
                    dve.drain().then_inc(bias_used, 1)
                    if half == 0:
                        left_lo(yThi, yTlo, chunks=4, order=from_residues if b == 1 else in_order)
                    split_to(c.unit + 3)
                    uses = slot_uses(c, halves=1)
                    split_to(c.unit + 2)
                    for t in range(TOK):
                        dve.wait_ge(sig_done, c.tick("sig"))
                        dve.wait_ge(bank_full[t], uses[t])
                        ms = merged[:, t, half * 512:half * 512 + 512]
                        if c.n["bg"] <= 2:
                            v.tensor_tensor(ms, bank[t][:, :], gbuf[:, t, :], ALU.mult).then_inc(bank_free[t], 1)
                            dve.wait_ge(bank_free[t], uses[t])
                        else:
                            v.tensor_tensor(gbuf[:, t, :], bank[t][:, :], gbuf[:, t, :], ALU.mult)\
                                .then_inc(bank_free[t], 1)
                            dve.wait_ge(bank_free[t], uses[t])
                            link(v.tensor_tensor(ms, ms, gbuf[:, t, :], ALU.add))

            c.turns = []
            dve.wait_ge(s_rope2, 16)
            for g in range(3):
                rotated_slot()
                rotated_slot()
                slot_uses(c)
                split_to(c.unit + 3)
                dve.wait_ge(s_mask, 16 * (g + 1))

                def keep(j, o):
                    h, i = DIL[j]
                    return v.tensor_copy(Og[:, g, i * 512 + h * DH2:i * 512 + h * DH2 + DH2], o)

                attention(DIL, lambda i: dil_span(g, i), DH2, lambda j: g * 32 + DIL[j][1] * 8 + DIL[j][0],
                          (lambda i, w: mask2[:, SEQ - w:SEQ]), SCALE2, keep)
                if g < 2:
                    milestone()
            mg = [ast2[:, 0, 32 * g:32 * g + 32] for g in range(3)]
            dve.wait_ge(bank_free[6], c.uses[6])
            dve.wait_ge(bank_free[7], c.uses[7])
            dve.wait_ge(s_residue, 16 * 2 * TOK * TOK)
            note(v.tensor_copy(ast2[:, 0, 0:32], stat0[:, 0, :]))
            link(v.tensor_copy(ast2[:, 2, 0:32], stat0[:, 1, :]))
            link(v.tensor_tensor(ast2[:, 5, 0:32], mg[0], mg[1], ALU.max))
            link(v.tensor_tensor(ast2[:, 5, 0:32], ast2[:, 5, 0:32], mg[2], ALU.max))
            for g in range(3):
                ins = v.tensor_tensor(ast2[:, 3, 32 * g:32 * g + 32], mg[g], ast2[:, 5, 0:32], ALU.subtract)
                if g < 2:
                    note(ins)
            ins.then_inc(shifted, 1)
            dve.wait_ge(raised, 1)
            link(v.tensor_tensor(ast2[:, 6, :], ast2[:, 4, :], ast2[:, 2, :], ALU.mult))
            link(v.tensor_tensor(ast2[:, 5, 0:32], ast2[:, 6, 0:32], ast2[:, 6, 32:64], ALU.add))
            link(v.tensor_tensor(ast2[:, 5, 0:32], ast2[:, 5, 0:32], ast2[:, 6, 64:96], ALU.add))
            link(v.reciprocal(ast2[:, 5, 32:64], ast2[:, 5, 0:32]))
            for g in range(3):
                note(v.tensor_tensor(ast2[:, 7, 32 * g:32 * g + 32], ast2[:, 4, 32 * g:32 * g + 32],
                                     ast2[:, 5, 32:64], ALU.mult))
            settle()
            for g in range(3):
                og_ = (Og[:, g, :] if g else y2[:, :, :].rearrange("p t n -> p (t n)")).rearrange(
                    "p (a d) -> p a d", d=DH2)
                note(v.tensor_tensor(og_, og_, ast2[:, 7, 32 * g:32 * g + 32].unsqueeze(2).to_broadcast([P, 32, DH2]),
                                     ALU.mult))
            settle()
            link(v.tensor_tensor(Og[:, 1, :], Og[:, 1, :], Og[:, 2, :], ALU.add))
            for t in range(TOK):
                v.tensor_tensor(y2[:, t, :], y2[:, t, :], Og[:, 1, 512 * t:512 * t + 512], ALU.add).then_inc(y_done, 1)
            merge(1)
            milestone()

            rotated_slot(side=True, doubled=2)
            rotated_slot(n=DH2, halves=1, side=True, doubled=1)
            rotated_slot()
            dve.wait_ge(s_mask, 16 * 4)
            link(v.tensor_copy(selb[:, 0, 0:P], mask2[:, SEQ - P:SEQ]))
            n = 0
            for i in range(1, TOK):
                w = (i + 1) * P
                sc = score[i - 1][:, 0:w]
                for h in range(4):
                    dve.wait_ge(bank_free[h], c.take(h))
                    if h == 0:
                        ins = v.tensor_scalar(sc, relu[:, h % 2, 0:w], iw[:, i, h:h + 1], None, ALU.mult)
                    else:
                        ins = v.scalar_tensor_tensor(out=sc, in0=relu[:, h % 2, 0:w], scalar=iw[:, i, h:h + 1], in1=sc,
                                                     op0=ALU.mult, op1=ALU.add)
                    ins.then_inc(relu_used, 1)
                    n += 1
                    dve.wait_ge(relu_used, n)
                link(v.tensor_tensor(sc, sc, mask2[:, SEQ - w:SEQ], ALU.add))

            def select(j):
                i, m = SELA[j][1] + 1, SELA[j][0]
                if i == TOK:
                    return
                w = (i + 1) * P
                sc = score[i - 1][:, 0:w]
                for _ in range(TOPK // 64):
                    link(v.max(sel8[:, :], sc))
                    link(v.match_replace(sc, sel8[:, :], sc, PICKED))
                if m == 7:
                    link(v.tensor_scalar(sc, sc, PICKED / 3, NEG, ALU.is_gt, ALU.mult))
                    link(v.tensor_tensor(selb[:, i, 0:w], sc, mask2[:, SEQ - w:SEQ], ALU.add))

            attention(SELA, lambda i: (0, (i + 1) * P), DH2, lambda j: j, lambda i, w: selb[:, i, 0:w], SCALE2,
                      divided(SELA, DH2), select)
            dve.wait_ge(bank_free[7], c.uses[7])
            for t in range(TOK):
                dve.drain().then_inc(y_done, 1)
            milestone()
            merge(0)
            milestone()

            dve.wait_ge(s_mem, 16)
            mean_roots(2, D)
            for t in range(2):
                v.tensor_scalar(memx[:, t, :], memx[:, t, :], stat[:, 2, t:t + 1], None, ALU.mult).then_inc(xn_done, 1)
            for n, tiles in enumerate((4, 4, 2)):
                slot_uses(c, tiles)
                split_to(c.unit + 3)
                if n == 0:
                    left_lo(memhi, memlo, 2 * LAYERS + 2, n=MEM)
            attention(MEMA, lambda i: (0, MEM), P, lambda j: j, None, SCALE_M, divided(MEMA, P))
            dve.wait_ge(bank_free[7], c.uses[7])
            for t in range(TOK):
                dve.drain().then_inc(y_done, 1)
            merge(2)
            milestone()
            left_lo(nThi, nTlo)
            add_to_x(0)
            add_to_x(1)
            dve.wait_ge(*c.x[-1])

            dve.wait_ge(wr_hi, 1)
            v.tensor_tensor(wrlo[:, :, :], wr[:, :, :], wrhi[:, :, :].bitcast(F32), ALU.subtract).then_inc(wr_lo, 1)
            norm(2 * LAYERS + 1)
            c.take(0)
            for t in range(TOK):
                dve.wait_ge(bank_full[t], c.take(t))
                v.tensor_tensor(sl[:, t, :], bank[t][:, 0:ROUTES], rb[:, :], ALU.add).then_inc(bank_free[t], 1)
            dve.wait_ge(bank_free[3], c.uses[3])

            def each(r, w=4):
                return rt[:, r, :, 0:w]

            def over(a, w=4):
                return a.to_broadcast([P, TOK, w])

            def first_best(src, best, hot, seen):
                link(v.tensor_reduce(each(best, 1), src, AX.X, ALU.max))
                link(v.tensor_tensor(each(hot), src, over(each(best, 1)), ALU.is_ge))
                link(v.tensor_scalar(each(seen, 1), rt[:, hot, :, 0:1], -1.0, 1.0, ALU.mult, ALU.add))
                for j in range(1, 4):
                    link(v.tensor_tensor(rt[:, hot, :, j:j + 1], rt[:, hot, :, j:j + 1], each(seen, 1), ALU.mult))
                    link(v.tensor_tensor(each(seen, 1), each(seen, 1), rt[:, hot, :, j:j + 1], ALU.subtract))

            first_best(sl[:, :, 0:4], 2, 3, 4)
            v.tensor_tensor(each(0), sl[:, :, 0:4], over(each(2, 1)), ALU.subtract).then_inc(shifted, 1)
            dve.wait_ge(raised, 2)
            link(v.tensor_reduce(each(5, 1), each(1), AX.X, ALU.add))
            link(v.reciprocal(each(5, 1), each(5, 1)))
            for g in range(4):
                link(v.tensor_tensor(each(6 if g == 0 else 7), sl[:, :, 4 + 4 * g:8 + 4 * g],
                                     over(rt[:, 3, :, g:g + 1]), ALU.mult))
                if g:
                    link(v.tensor_tensor(each(6), each(6), each(7), ALU.add))
            first_best(each(6), 10, 11, 4)
            link(v.scalar_tensor_tensor(out=each(7), in0=each(11), scalar=PICKED, in1=each(6), op0=ALU.mult,
                                        op1=ALU.add))
            first_best(each(7), 12, 13, 4)
            v.tensor_tensor(each(8, 1), each(12, 1), each(10, 1), ALU.subtract).then_inc(shifted, 1)
            dve.wait_ge(raised, 3)
            link(v.tensor_scalar(each(14, 1), each(9, 1), 1.0, None, ALU.add))
            link(v.reciprocal(each(14, 1), each(14, 1)))
            link(v.tensor_tensor(each(14, 1), each(14, 1), each(5, 1), ALU.mult))
            link(v.tensor_tensor(each(15, 1), each(14, 1), each(9, 1), ALU.mult))
            for g in range(4):
                gs = over(rt[:, 3, :, g:g + 1])
                note(v.tensor_tensor(ep[:, 0, :, 4 * g:4 * g + 4], each(11), gs, ALU.mult))
                note(v.tensor_tensor(ep[:, 1, :, 4 * g:4 * g + 4], each(13), gs, ALU.mult))
            settle()
            v.tensor_tensor(ep[:, 2, :, :], ep[:, 0, :, :], ep[:, 1, :, :], ALU.add).then_inc(member, 1)
            dve.wait_ge(s_tables, 16 * 3)
            for b in range(2):
                dve.wait_ge(bank_full[b], c.take(b))
            v.tensor_copy(ep[:, 4, :, :], bank[1][:, 0:TOK * EXPERTS].rearrange("p (t e) -> p t e", e=EXPERTS))\
                .then_inc(bank_free[1], 1)
            dve.wait_ge(bank_free[1], c.uses[1])
            link(v.tensor_reduce(ch[:, 0, :], ep[:, 4, :, :].rearrange("p t e -> p e t"), AX.X, ALU.add))
            link(v.tensor_scalar(ch[:, 1, :], ch[:, 0, :], 0.0, None, ALU.is_gt))
            for n in range(1, TOK):
                link(v.scalar_tensor_tensor(out=ch[:, 1, :], in0=ch[:, 0, :], scalar=float(n * P), in1=ch[:, 1, :],
                                            op0=ALU.is_gt, op1=ALU.add))
            at_ = 1
            for level in range(4):
                n, to = 2 ** level, 2 + level % 2
                note(v.tensor_copy(ch[:, to, 0:n], ch[:, at_, 0:n]))
                link(v.tensor_tensor(ch[:, to, n:EXPERTS], ch[:, at_, n:EXPERTS], ch[:, at_, 0:EXPERTS - n], ALU.add))
                at_ = to
            end = ch[:, at_, :]
            link(v.tensor_tensor(ch[:, 4, :], end, ch[:, 1, :], ALU.subtract))
            link(v.tensor_scalar(ch[:, 4, :], ch[:, 4, :], float(P), None, ALU.mult))
            for t in range(TOK):
                ins = v.tensor_tensor(ep[:, 3, t, :], bank[0][:, t * EXPERTS:(t + 1) * EXPERTS], ch[:, 4 + t, :], ALU.add)
                if t < TOK - 1:
                    note(ins)
                    link(v.tensor_tensor(ch[:, 5 + t, :], ch[:, 4 + t, :], ep[:, 4, t, :], ALU.add))
            ins.then_inc(bank_free[0], 1)
            dve.wait_ge(bank_free[0], c.uses[0])
            for k in range(2):
                link(v.tensor_tensor(ep[:, 4, :, :], ep[:, k, :, :], ep[:, 3, :, :], ALU.mult))
                link(v.tensor_reduce(spot[:, k, :], ep[:, 4, :, :], AX.X, ALU.add))
            R = [rel[:, k, :].rearrange("p (t n) -> p t n", n=CHUNKS) for k in range(5)]
            for k in range(2):
                link(v.tensor_tensor(R[0], spot[:, k, :].unsqueeze(2).to_broadcast([P, TOK, CHUNKS]),
                                     steps[:, 0, :].unsqueeze(1).to_broadcast([P, TOK, CHUNKS]), ALU.subtract))
                link(v.tensor_scalar(R[1], R[0], 0.0, None, ALU.is_ge))
                link(v.scalar_tensor_tensor(out=rel[:, 1, :], in0=rel[:, 0, :], scalar=float(P), in1=rel[:, 1, :],
                                            op0=ALU.is_lt, op1=ALU.mult))
                weight = each(14 + k, 1).to_broadcast([P, TOK, CHUNKS])
                link(v.scalar_tensor_tensor(out=rel[:, 2 + k, :], in0=rel[:, 0, :], scalar=1.0, in1=rel[:, 1, :],
                                            op0=ALU.add, op1=ALU.mult))
                if k == 0:
                    link(v.tensor_tensor(wts[:, :, :], R[1], weight, ALU.mult))
                else:
                    link(v.tensor_tensor(R[4], R[1], weight, ALU.mult))
            note(v.tensor_tensor(wts[:, :, :], wts[:, :, :], R[4], ALU.add))
            link(v.tensor_tensor(R[2], R[2], R[3], ALU.add))
            link(v.tensor_scalar(keys[:, :, :], R[2], -1.0, None, ALU.add))
            link(v.tensor_tensor(ecmp[:, :, :], end.unsqueeze(1).to_broadcast([P, CHUNKS, EXPERTS]),
                                 steps[:, 1, :].unsqueeze(2).to_broadcast([P, CHUNKS, EXPERTS]), ALU.is_le))
            note(v.tensor_copy(efl[:, CHUNKS:CHUNKS + 1], end[:, EXPERTS - 1:EXPERTS]))
            link(v.tensor_reduce(efl[:, 0:CHUNKS], ecmp[:, :, :], AX.X, ALU.add))
            link(v.tensor_scalar(efl[:, 0:CHUNKS], efl[:, 0:CHUNKS], float(EXPERTS - 1), None, ALU.min))
            v.tensor_copy(ids[:, :], efl[:, :]).then_inc(placed, 1)
            dve.wait_ge(placed, 1)
            chunks = v.value_load(ids[0:1, CHUNKS:CHUNKS + 1], min_val=SEQ * 2 // P, max_val=CHUNKS - 1)
            u, U, N = list(c.uses), c.unit, c.n["nhi"]

            def full(b, n):
                dve.wait_ge(bank_full[b], u[b] + n)

            def one_hots(i):
                at_i = slice(i, i + 1) if isinstance(i, int) else bass.ds(i, 1)
                v.tensor_tensor(hot[:, :, :], slots[:, :].unsqueeze(1).to_broadcast([P, TOK, P]),
                                keys[:, :, at_i].to_broadcast([P, TOK, P]), ALU.is_equal).then_inc(hot_done, 1)

            def split_unit(i, j):
                dve.wait_ge(hi_done, U + 6 * i + j + 1)
                hi, lo = parts(U, j)
                v.tensor_tensor(lo, raw[:, (U + j) % RING, :], hi.bitcast(F32), ALU.subtract).then_inc(split_done, 1)

            def gathered(i, halves=(0, 1)):
                for k in halves:
                    dve.wait_ge(nhi_done, N + 2 * i + k + 1)
                    for j in range(4 * k, 4 * k + 4):
                        lo = v.scalar_tensor_tensor(out=xglo[:, j, :], in0=bank[2 + k][:, (j % 4) * P:(j % 4) * P + P],
                                                    scalar=gcol[:, 2 * LAYERS + 1, j:j + 1],
                                                    in1=xghi[:, j, :].bitcast(F32), op0=ALU.mult, op1=ALU.subtract)
                    lo.then_inc(bank_free[2 + k], 1)

            def add_chunk(i):
                dve.wait_ge(bank_free[3], u[3] + 4 * i - 2)
                at_i = bass.ds(i - 1, 1)
                for j in range(8):
                    t, half, b = j // 2, j % 2, 2 + j % 3
                    full(b, (3 * i - 1 if b == 4 else 4 * i - 1) + j // 3)
                    xs = x[:, t, half * 512:half * 512 + 512]
                    v.scalar_tensor_tensor(out=xs, in0=bank[b][:, :], scalar=wts[:, t, at_i], in1=xs,
                                           op0=ALU.mult, op1=ALU.add).then_inc(bank_free[b], 1)

            def chunk(i):
                split_unit(i, 5)
                full(5, i + 1)
                one_hots(i + 1)
                split_unit(i, 6)
                split_unit(i, 7)
                dve.wait_ge(bank_free[0], u[0] + i + 1)
                full(1, i + 1)
                v.tensor_tensor(mh[:, :], bank[1][:, :], msg[:, :], ALU.mult).then_inc(bank_free[1], 1)
                if not isinstance(i, int):
                    add_chunk(i)
                dve.wait_ge(ht_hi, i + 1)
                v.tensor_tensor(htlo[:, :, :].rearrange("p k n -> p (k n)"), bank[4][:, :],
                                hthi[:, :, :].rearrange("p k n -> p (k n)").bitcast(F32), ALU.subtract)\
                    .then_inc(bank_free[4], 1)
                split_unit(i, 8)
                gathered(i + 1, (0,))
                split_unit(i, 9)
                gathered(i + 1, (1,))
                split_unit(i, 10)
                for b in (6, 7):
                    dve.wait_ge(y_hi, 2 * i + b - 5)
                    cs = slice((b - 6) * 512, (b - 6) * 512 + 512)
                    v.tensor_tensor(ylo[:, cs], bank[b][:, :], yhi[:, cs].bitcast(F32), ALU.subtract)\
                        .then_inc(bank_free[b], 1)

            one_hots(0)
            for j in range(5):
                if j == 2:
                    gathered(0)
                split_unit(0, j)
            chunk(0)
            with dve.Fori(1, chunks) as i:
                chunk(i)
            add_chunk(chunks)
            dve.drain().then_inc(x_final, 1)

            mean_roots(TOK, D)
            dve.wait_ge(s_g, 16)
            for t in range(TOK):
                v.scalar_tensor_tensor(out=xn[:, t, :], in0=x[:, t, :], scalar=stat[:, 2, t:t + 1], in1=og[:, :],
                                       op0=ALU.mult, op1=ALU.mult).then_inc(out_done, 1)


_INS = ["x", "w_in", "q_norm_g", "k_norm_g", "lam_q1", "lam_k1", "lam_q2", "lam_k2", "subln_g", "pool_w", "pool_scale",
        "w_out", "w_ffn_in", "w_ffn_out", "mem_2", "w_in_2", "w_mem_kv_2", "w_gate_2", "b_gate_2", "w_branch_2",
        "w_out_2", "w_group_2", "b_group_2", "w_sub_2", "b_sub_2", "w1_2", "w3_2", "w2_2", "g_final_2"]


def kernel(**inputs):
    import concourse.bacc as bacc
    from concourse.bass_utils import run_bass_kernel_spmd

    arrays = {name: np.ascontiguousarray(inputs[name]) for name in _INS}
    gains = [np.asarray(inputs[n])[l] for l in range(LAYERS) for n in ("norm1_g", "norm2_g")]
    gains += [np.asarray(inputs[n])[0] for n in ("g_mix_2", "g_ffn_2", "g_mem_2")]
    arrays["c_gains"] = np.ascontiguousarray(np.stack([g.reshape(KT, P).T for g in gains], axis=1))
    arrays.update(host_constants())
    nc = bacc.Bacc("TRN2", target_bir_lowering=False, num_devices=1)
    A = {n: nc.dram_tensor("in_" + n, a.shape, mybir.dt.from_np(a.dtype), kind="ExternalInput").ap()
         for n, a in arrays.items()}
    out = nc.dram_tensor("out", (1, SEQ, D), F32, kind="ExternalOutput").ap()
    build(nc, A, out)
    r = run_bass_kernel_spmd(nc, [{"in_" + n: a for n, a in arrays.items()}], core_ids=[0])
    return r.results[0]["out"]
```
